# Optimizing a Trainium2 kernel written in Bass

```python
import math
import jax, jax.numpy as jnp
from jax import lax
import numpy as np

D_MODEL = 1024
BATCH = 1
SEQ = 512
DEPTH = 1

GRID_W = 64
CTX_LEN = 256
N_MOD = 6
EPS = 1e-6

F_GROUPS = 8
F_GROUP_DIM = 128
F_WIDTH = F_GROUPS * F_GROUP_DIM

D_INNER = 2 * D_MODEL
HEAD_DIM = 64
N_HEADS = D_INNER // HEAD_DIM
N_GROUPS = 4
HEADS_PER_GROUP = N_HEADS // N_GROUPS
D_STATE = 128
BC_WIDTH = N_GROUPS * D_STATE
CONV_K = 5
CHUNK = 128

N_EXPERTS = 32
TOP_K = 4
D_FF = D_MODEL
SWIGLU_LIMIT = 7.0
SWIGLU_ALPHA = 1.702
MOE_BLOCK = 128

OFF_X = 0
OFF_BF = OFF_X + D_INNER
OFF_BB = OFF_BF + BC_WIDTH
OFF_DT = OFF_BB + BC_WIDTH
OFF_CF = OFF_DT + 2 * N_HEADS
OFF_CB = OFF_CF + BC_WIDTH
OFF_Z = OFF_CB + BC_WIDTH
OFF_F = OFF_Z + D_INNER
OFF_GF = OFF_F + F_WIDTH
OFF_GS = OFF_GF + D_MODEL
IN_COLS = OFF_GS + D_MODEL
XB_CH = OFF_DT
CONV_CH = XB_CH + 2 * BC_WIDTH


def rmsnorm(v, w):
    v32 = v.astype(jnp.float32)
    inv = lax.rsqrt(jnp.mean(v32 * v32, axis=-1, keepdims=True) + EPS)
    return (v32 * inv * w.astype(jnp.float32)).astype(v.dtype)

def dwconv_centred(u, w, bias):
    ch = u.shape[-1]
    y = lax.conv_general_dilated(u, w[:, None, :].astype(u.dtype), window_strides=(1,),
                                 padding=[(CONV_K // 2, CONV_K // 2)],
                                 dimension_numbers=('NWC', 'WIO', 'NWC'),
                                 feature_group_count=ch)
    return y + bias

def _decay_matrix(a_cs):
    q = a_cs.shape[-1]
    mask = jnp.tril(jnp.ones((q, q), dtype=bool))
    diff = a_cs[..., :, None] - a_cs[..., None, :]
    return jnp.exp(jnp.where(mask, diff, -jnp.inf))

def _ssd_chunks(x, dt, a, b_in):
    bsz, l = x.shape[:2]
    nc = l // CHUNK
    a_cs = jnp.cumsum((dt * a).reshape(bsz, nc, CHUNK, N_GROUPS, HEADS_PER_GROUP), axis=2)
    xdt = (x.astype(jnp.float32) * dt[..., None]).reshape(bsz, nc, CHUNK, N_GROUPS, HEADS_PER_GROUP, HEAD_DIM)
    bc = b_in.astype(jnp.float32).reshape(bsz, nc, CHUNK, N_GROUPS, D_STATE)
    decay_to_end = jnp.exp(a_cs[:, :, -1:] - a_cs)
    states = jnp.einsum('bcsgn,bcsgh,bcsghp->bcghpn', bc, decay_to_end, xdt)
    chunk_decay = jnp.exp(a_cs[:, :, -1])
    return a_cs, xdt, bc, states, chunk_decay

def _carry_states(states, chunk_decay, h0):
    def step(h, inp):
        s, dec = inp
        return h * dec[..., None, None] + s, h
    h_final, h_prev = lax.scan(step, h0, (jnp.moveaxis(states, 1, 0), jnp.moveaxis(chunk_decay, 1, 0)))
    return jnp.moveaxis(h_prev, 0, 1), h_final

def ssd_final_state(x, dt, a, b_in, h0):
    _, _, _, states, chunk_decay = _ssd_chunks(x, dt, a, b_in)
    return _carry_states(states, chunk_decay, h0)[1]

def ssd_scan(x, dt, a, b_in, c_in, h0):
    bsz, l = x.shape[:2]
    nc = l // CHUNK
    a_cs, xdt, bc, states, chunk_decay = _ssd_chunks(x, dt, a, b_in)
    h_prev, _ = _carry_states(states, chunk_decay, h0)
    cc = c_in.astype(jnp.float32).reshape(bsz, nc, CHUNK, N_GROUPS, D_STATE)
    decay_in = _decay_matrix(jnp.moveaxis(a_cs, 2, -1))
    cb = jnp.einsum('bclgn,bcsgn->bcgls', cc, bc)
    y_diag = jnp.einsum('bcgls,bcghls,bcsghp->bclghp', cb, decay_in, xdt)
    y_off = jnp.einsum('bclgn,bcghpn,bclgh->bclghp', cc, h_prev, jnp.exp(a_cs))
    return (y_diag + y_off).reshape(bsz, l, N_HEADS, HEAD_DIM)

def moe_ffn(h, w_router, b_router, w_gate_up, b_gate_up, w_down, b_down):
    bsz, n, d = h.shape
    tok = h.reshape(-1, d)
    n_tok = tok.shape[0]
    logits = (tok @ w_router + b_router).astype(jnp.float32)
    top_logit, top_idx = lax.top_k(logits, TOP_K)
    top_w = jax.nn.softmax(top_logit, axis=-1)
    flat_e = top_idx.reshape(-1)
    flat_w = top_w.reshape(-1)
    n_assign = flat_e.shape[0]
    order = jnp.argsort(flat_e)
    e_sorted = flat_e[order]
    tok_sorted = (order // TOP_K).astype(jnp.int32)
    counts = jnp.bincount(flat_e, length=N_EXPERTS)
    padded = (counts + MOE_BLOCK - 1) // MOE_BLOCK * MOE_BLOCK
    pad_end = jnp.cumsum(padded)
    pad_start = pad_end - padded
    start = jnp.cumsum(counts) - counts
    dest = pad_start[e_sorted] + jnp.arange(n_assign) - start[e_sorted]
    n_blocks = (n_assign + MOE_BLOCK - 1) // MOE_BLOCK + N_EXPERTS
    rows = n_blocks * MOE_BLOCK
    row_tok = jnp.full((rows,), n_tok, jnp.int32).at[dest].set(tok_sorted)
    row_w = jnp.zeros((rows,), jnp.float32).at[dest].set(flat_w[order])
    blk_e = jnp.minimum(jnp.searchsorted(pad_end, jnp.arange(n_blocks) * MOE_BLOCK, side='right'),
                        N_EXPERTS - 1)
    tok_ext = jnp.concatenate([tok, jnp.zeros((1, d), tok.dtype)], axis=0)
    xb = tok_ext[row_tok].reshape(n_blocks, MOE_BLOCK, d)

    def expert_block(args):
        xe, e = args
        gu = xe @ w_gate_up[e] + b_gate_up[e]
        gate = jnp.minimum(gu[:, :D_FF], SWIGLU_LIMIT)
        up = jnp.clip(gu[:, D_FF:], -SWIGLU_LIMIT, SWIGLU_LIMIT)
        act = (up + 1.0) * gate * jax.nn.sigmoid(SWIGLU_ALPHA * gate)
        return act @ w_down[e] + b_down[e]

    yb = lax.map(expert_block, (xb, blk_e)).reshape(rows, d)
    yb = yb * row_w[:, None].astype(yb.dtype)
    out = jnp.zeros_like(tok_ext).at[row_tok].add(yb)[:n_tok]
    return out.reshape(bsz, n, d)

def first_inputs(seed: int = 0) -> dict:
    key = jax.random.key(seed)
    ks = jax.random.split(key, 25)
    f32 = jnp.float32
    D = D_MODEL

    def nrm(k, shape, scale):
        return jax.random.normal(k, shape, f32) * scale

    dt0 = jnp.exp(jax.random.uniform(ks[11], (DEPTH, 2, N_HEADS), f32, math.log(1e-3), math.log(1e-1)))
    return {
        'x': nrm(ks[0], (BATCH, SEQ, D), 1.0),
        'c': nrm(ks[1], (BATCH, D), 1.0),
        'ctx': nrm(ks[2], (BATCH, CTX_LEN, D), 1.0),
        'c_ctx': nrm(ks[3], (D,), 1.0),
        'w_mod': nrm(ks[4], (DEPTH, D, N_MOD * D), 0.5 * D ** -0.5),
        'b_mod': nrm(ks[5], (DEPTH, N_MOD * D), 0.02),
        'norm1_w': 1.0 + nrm(ks[6], (DEPTH, D), 0.05),
        'norm2_w': 1.0 + nrm(ks[7], (DEPTH, D), 0.05),
        'w_in': nrm(ks[8], (DEPTH, D, IN_COLS), D ** -0.5),
        'conv_w': nrm(ks[9], (DEPTH, CONV_K, CONV_CH), CONV_K ** -0.5),
        'conv_b': nrm(ks[10], (DEPTH, CONV_CH), 0.02),
        'dt_bias': dt0 + jnp.log(-jnp.expm1(-dt0)),
        'a_log': jnp.log(jax.random.uniform(ks[12], (DEPTH, 2, N_HEADS), f32, 1.0, 16.0)),
        'd_skip': 1.0 + nrm(ks[13], (DEPTH, N_HEADS), 0.1),
        'ssd_norm_w': 1.0 + nrm(ks[14], (DEPTH, D_INNER), 0.05),
        'w_ssd_out': nrm(ks[15], (DEPTH, D_INNER, D), D_INNER ** -0.5),
        'w_four_out': nrm(ks[16], (DEPTH, F_WIDTH, D), F_WIDTH ** -0.5),
        'w_o': nrm(ks[17], (DEPTH, D, D), D ** -0.5),
        'w_router': nrm(ks[18], (DEPTH, D, N_EXPERTS), D ** -0.5),
        'b_router': nrm(ks[19], (DEPTH, N_EXPERTS), 0.01),
        'w_gate_up': nrm(ks[20], (DEPTH, N_EXPERTS, D, 2 * D_FF), D ** -0.5),
        'b_gate_up': nrm(ks[21], (DEPTH, N_EXPERTS, 2 * D_FF), 0.02),
        'w_down': nrm(ks[22], (DEPTH, N_EXPERTS, D_FF, D), D_FF ** -0.5),
        'b_down': nrm(ks[23], (DEPTH, N_EXPERTS, D), 0.02),
        'final_norm_w': 1.0 + nrm(ks[24], (D,), 0.05),
    }

def first_block(x, c, ctx, c_ctx, w_mod, b_mod, norm1_w, norm2_w, w_in, conv_w, conv_b, dt_bias,
              a_log, d_skip, ssd_norm_w, w_ssd_out, w_four_out, w_o, w_router, b_router,
              w_gate_up, b_gate_up, w_down, b_down, final_norm_w):
    bsz, n, D = x.shape
    n_ctx = ctx.shape[1]
    h0 = jnp.zeros((bsz, N_GROUPS, HEADS_PER_GROUP, HEAD_DIM, D_STATE), jnp.float32)
    for layer in range(DEPTH):
        mod = jax.nn.silu(c) @ w_mod[layer] + b_mod[layer]
        sh1, sc1, g1, sh2, sc2, g2 = jnp.split(mod[:, None, :], N_MOD, axis=-1)
        mod_c = jax.nn.silu(c_ctx) @ w_mod[layer][:, :2 * D] + b_mod[layer][:2 * D]
        sh1_c, sc1_c = mod_c[:D], mod_c[D:]
        a = -jnp.exp(a_log[layer].astype(jnp.float32))

        hc = rmsnorm(ctx, norm1_w[layer]) * (1.0 + sc1_c) + sh1_c
        pc = hc @ w_in[layer][:, :OFF_CF]
        xb_c = jax.nn.silu(dwconv_centred(pc[..., :XB_CH], conv_w[layer][:, :XB_CH], conv_b[layer][:XB_CH]))
        xc = xb_c[..., :D_INNER].reshape(bsz, n_ctx, N_HEADS, HEAD_DIM)
        bfc = xb_c[..., OFF_BF:OFF_BB].reshape(bsz, n_ctx, N_GROUPS, D_STATE)
        bbc = xb_c[..., OFF_BB:OFF_DT].reshape(bsz, n_ctx, N_GROUPS, D_STATE)
        dtc = jax.nn.softplus(pc[..., OFF_DT:OFF_CF].astype(jnp.float32).reshape(bsz, n_ctx, 2, N_HEADS)
                              + dt_bias[layer].astype(jnp.float32))
        hf_ctx = ssd_final_state(xc, dtc[:, :, 0], a[0], bfc, h0)
        hb_ctx = ssd_final_state(xc[:, ::-1], dtc[:, ::-1, 1], a[1], bbc[:, ::-1], h0)

        h = rmsnorm(x, norm1_w[layer]) * (1.0 + sc1) + sh1
        p = h @ w_in[layer]

        xl = jax.nn.silu(dwconv_centred(p[..., :XB_CH], conv_w[layer][:, :XB_CH], conv_b[layer][:XB_CH]))
        cl = jax.nn.silu(dwconv_centred(p[..., OFF_CF:OFF_Z], conv_w[layer][:, XB_CH:], conv_b[layer][XB_CH:]))
        xs = xl[..., :D_INNER].reshape(bsz, n, N_HEADS, HEAD_DIM)
        bf = xl[..., OFF_BF:OFF_BB].reshape(bsz, n, N_GROUPS, D_STATE)
        bb = xl[..., OFF_BB:OFF_DT].reshape(bsz, n, N_GROUPS, D_STATE)
        cf = cl[..., :BC_WIDTH].reshape(bsz, n, N_GROUPS, D_STATE)
        cb = cl[..., BC_WIDTH:].reshape(bsz, n, N_GROUPS, D_STATE)
        dtl = jax.nn.softplus(p[..., OFF_DT:OFF_CF].astype(jnp.float32).reshape(bsz, n, 2, N_HEADS)
                              + dt_bias[layer].astype(jnp.float32))
        y_f = ssd_scan(xs, dtl[:, :, 0], a[0], bf, cf, hf_ctx)
        y_b = ssd_scan(xs[:, ::-1], dtl[:, ::-1, 1], a[1], bb[:, ::-1], cb[:, ::-1], hb_ctx)[:, ::-1]
        y = y_f + y_b + d_skip[layer].astype(jnp.float32)[:, None] * xs.astype(jnp.float32)
        y = y.reshape(bsz, n, D_INNER).astype(x.dtype)
        z = p[..., OFF_Z:OFF_F]
        y_ssd = rmsnorm(y * jax.nn.silu(z), ssd_norm_w[layer]) @ w_ssd_out[layer]

        u = p[..., OFF_F:OFF_GF].astype(jnp.float32).reshape(bsz, n, F_GROUPS, F_GROUP_DIM)
        u = jnp.fft.fft2(u, axes=(1, 3), norm='ortho').real.reshape(bsz, n, F_WIDTH).astype(x.dtype)
        y_four = u @ w_four_out[layer]

        gate_f = jax.nn.sigmoid(p[..., OFF_GF:OFF_GS])
        gate_s = jax.nn.sigmoid(p[..., OFF_GS:IN_COLS])
        mix = (gate_f * y_four + gate_s * y_ssd) @ w_o[layer]
        x = x + g1 * mix

        h2 = rmsnorm(x, norm2_w[layer]) * (1.0 + sc2) + sh2
        x = x + g2 * moe_ffn(h2, w_router[layer], b_router[layer], w_gate_up[layer], b_gate_up[layer],
                             w_down[layer], b_down[layer])
    return rmsnorm(x, final_norm_w)


N_META = 16
HEAD_DIM_2 = 128
N_Q_HEADS = 8
N_KV_HEADS = 2
Q_GROUP = N_Q_HEADS // N_KV_HEADS
Q_WIDTH = N_Q_HEADS * HEAD_DIM_2
KV_WIDTH = N_KV_HEADS * HEAD_DIM_2
RNN_WIDTH = D_MODEL
RNN_BLOCKS = 8
RNN_BLOCK = RNN_WIDTH // RNN_BLOCKS
CONV_W = 4
CONV_PAD_L = CONV_W // 2
CONV_PAD_R = CONV_W - 1 - CONV_PAD_L
RG_C = 8.0
ROPE_THETA = 10000.0
ROPE_AXIS_DIM = HEAD_DIM_2 // 2
ROPE_PAIRS = ROPE_AXIS_DIM // 2
Q_BLOCK = 128
D_FF_2 = ((8 * D_MODEL + 3 * 256 - 1) // (3 * 256)) * 256
IN_WIDTH = Q_WIDTH + 2 * KV_WIDTH + 2 * RNN_WIDTH + 2 * D_MODEL


def rmsnorm_2(x, g):
    xf = x.astype(jnp.float32)
    y = xf * lax.rsqrt(jnp.mean(xf * xf, axis=-1, keepdims=True) + EPS)
    return (y * g.astype(jnp.float32)).astype(x.dtype)

def axial_rope_tables(n_tok):
    rows = n_tok // GRID_W
    row = jnp.repeat(jnp.arange(rows, dtype=jnp.float32), GRID_W)
    col = jnp.tile(jnp.arange(GRID_W, dtype=jnp.float32), rows)
    zeros = jnp.zeros((N_META,), jnp.float32)
    row = jnp.concatenate([zeros, row])
    col = jnp.concatenate([zeros, col])
    inv_freq = jnp.exp(-jnp.log(jnp.float32(ROPE_THETA)) * jnp.arange(ROPE_PAIRS, dtype=jnp.float32) / ROPE_PAIRS)
    ang_r = row[:, None] * inv_freq[None, :]
    ang_c = col[:, None] * inv_freq[None, :]
    return jnp.cos(ang_r), jnp.sin(ang_r), jnp.cos(ang_c), jnp.sin(ang_c)

def rotate_half_axis(xh, cos, sin):
    c = cos[None, :, None, :]
    s = sin[None, :, None, :]
    x1, x2 = xh[..., :ROPE_PAIRS], xh[..., ROPE_PAIRS:]
    return jnp.concatenate([x1 * c - x2 * s, x2 * c + x1 * s], axis=-1)

def apply_axial_rope(x, tabs):
    cos_r, sin_r, cos_c, sin_c = tabs
    xf = x.astype(jnp.float32)
    xr = rotate_half_axis(xf[..., :ROPE_AXIS_DIM], cos_r, sin_r)
    xc = rotate_half_axis(xf[..., ROPE_AXIS_DIM:], cos_c, sin_c)
    return jnp.concatenate([xr, xc], axis=-1).astype(x.dtype)

def bidirectional_gqa(q, k, v):
    B, T = q.shape[0], q.shape[1]
    q = q.reshape(B, T, N_KV_HEADS, Q_GROUP, HEAD_DIM_2)
    scale = HEAD_DIM_2 ** -0.5

    def block(qb):
        s = jnp.einsum('bqhgd,bkhd->bhgqk', qb, k, preferred_element_type=jnp.float32) * scale
        p = jax.nn.softmax(s, axis=-1)
        return jnp.einsum('bhgqk,bkhd->bqhgd', p.astype(v.dtype), v)

    q_meta, q_real = q[:, :N_META], q[:, N_META:]
    n_blk = q_real.shape[1] // Q_BLOCK
    qr = q_real.reshape(B, n_blk, Q_BLOCK, N_KV_HEADS, Q_GROUP, HEAD_DIM_2).transpose(1, 0, 2, 3, 4, 5)
    o_real = lax.map(block, qr)
    o_real = o_real.transpose(1, 0, 2, 3, 4, 5).reshape(B, n_blk * Q_BLOCK, Q_WIDTH)
    o_meta = block(q_meta).reshape(B, N_META, Q_WIDTH)
    return jnp.concatenate([o_meta, o_real], axis=1)

def centred_dwconv(x, w, b):
    T = x.shape[1]
    xp = jnp.pad(x, ((0, 0), (CONV_PAD_L, CONV_PAD_R), (0, 0)))
    y = b
    for j in range(CONV_W):
        y = y + xp[:, j:j + T] * w[j]
    return y

def _linear_recurrence_combine(e1, e2):
    a1, b1 = e1
    a2, b2 = e2
    return a1 * a2, a2 * b1 + b2

def rg_lru(xc, wa, ba, wx, bx, lam, reverse):
    B, T, C = xc.shape
    xf = xc.astype(jnp.float32)
    xb = xf.reshape(B, T, RNN_BLOCKS, RNN_BLOCK)
    r = jax.nn.sigmoid(jnp.einsum('btnc,ncd->btnd', xb, wa.astype(jnp.float32)).reshape(B, T, C) + ba.astype(jnp.float32))
    i = jax.nn.sigmoid(jnp.einsum('btnc,ncd->btnd', xb, wx.astype(jnp.float32)).reshape(B, T, C) + bx.astype(jnp.float32))
    log_a = RG_C * r * jax.nn.log_sigmoid(lam.astype(jnp.float32))
    a = jnp.exp(log_a)
    u = jnp.sqrt(-jnp.expm1(2.0 * log_a)) * (i * xf)
    _, h = lax.associative_scan(_linear_recurrence_combine, (a, u), axis=1, reverse=reverse)
    return h

def second_inputs(seed: int = 0) -> dict:
    key = jax.random.key(seed)
    ks = jax.random.split(key, 20)
    f32 = jnp.float32

    def nrm(k, shape, fan_in):
        return jax.random.normal(k, shape, f32) * (fan_in ** -0.5)

    x = jax.random.normal(ks[0], (BATCH, SEQ, D_MODEL), f32)
    meta_tokens = jax.random.normal(ks[1], (N_META, D_MODEL), f32)
    norm1_g = 1.0 + 0.05 * jax.random.normal(ks[2], (DEPTH, D_MODEL), f32)
    w_in = nrm(ks[3], (DEPTH, D_MODEL, IN_WIDTH), D_MODEL)
    conv_w = nrm(ks[4], (DEPTH, CONV_W, RNN_WIDTH), CONV_W)
    conv_b = 0.02 * jax.random.normal(ks[5], (DEPTH, RNN_WIDTH), f32)
    rg_wa = nrm(ks[6], (DEPTH, 2, RNN_BLOCKS, RNN_BLOCK, RNN_BLOCK), RNN_BLOCK)
    rg_ba = 0.02 * jax.random.normal(ks[7], (DEPTH, 2, RNN_WIDTH), f32)
    rg_wx = nrm(ks[8], (DEPTH, 2, RNN_BLOCKS, RNN_BLOCK, RNN_BLOCK), RNN_BLOCK)
    rg_bx = 0.02 * jax.random.normal(ks[9], (DEPTH, 2, RNN_WIDTH), f32)
    a_c = jax.random.uniform(ks[10], (DEPTH, 2, RNN_WIDTH), f32, 0.9, 0.999)
    s = a_c ** (1.0 / RG_C)
    rg_lambda = jnp.log(s) - jnp.log1p(-s)
    q_norm_g = 1.0 + 0.05 * jax.random.normal(ks[11], (DEPTH, HEAD_DIM_2), f32)
    k_norm_g = 1.0 + 0.05 * jax.random.normal(ks[12], (DEPTH, HEAD_DIM_2), f32)
    w_out = nrm(ks[13], (DEPTH, D_MODEL, D_MODEL), D_MODEL)
    norm2_g = 1.0 + 0.05 * jax.random.normal(ks[14], (DEPTH, D_MODEL), f32)
    w_ffn_in = nrm(ks[15], (DEPTH, D_MODEL, 2 * D_FF_2), D_MODEL)
    w_ffn_out = nrm(ks[16], (DEPTH, D_FF_2, D_MODEL), D_FF_2)
    return {'x': x, 'meta_tokens': meta_tokens, 'norm1_g': norm1_g, 'w_in': w_in,
            'conv_w': conv_w, 'conv_b': conv_b, 'rg_wa': rg_wa, 'rg_ba': rg_ba,
            'rg_wx': rg_wx, 'rg_bx': rg_bx, 'rg_lambda': rg_lambda,
            'q_norm_g': q_norm_g, 'k_norm_g': k_norm_g, 'w_out': w_out,
            'norm2_g': norm2_g, 'w_ffn_in': w_ffn_in, 'w_ffn_out': w_ffn_out}

def second_block(x, meta_tokens, norm1_g, w_in, conv_w, conv_b, rg_wa, rg_ba, rg_wx, rg_bx,
              rg_lambda, q_norm_g, k_norm_g, w_out, norm2_g, w_ffn_in, w_ffn_out):
    B, S, D = x.shape
    meta = jnp.broadcast_to(meta_tokens.astype(x.dtype)[None], (B, N_META, D))
    h = jnp.concatenate([meta, x], axis=1)
    T = h.shape[1]
    tabs = axial_rope_tables(S)
    splits = [Q_WIDTH, Q_WIDTH + KV_WIDTH, Q_WIDTH + 2 * KV_WIDTH,
              Q_WIDTH + 2 * KV_WIDTH + RNN_WIDTH, Q_WIDTH + 2 * KV_WIDTH + 2 * RNN_WIDTH]

    for l in range(DEPTH):
        xn = rmsnorm_2(h, norm1_g[l])
        proj = xn @ w_in[l]
        q, k, v, xr, gr, g_merge = jnp.split(proj, splits, axis=-1)

        q = q.reshape(B, T, N_Q_HEADS, HEAD_DIM_2)
        k = k.reshape(B, T, N_KV_HEADS, HEAD_DIM_2)
        v = v.reshape(B, T, N_KV_HEADS, HEAD_DIM_2)
        q = apply_axial_rope(rmsnorm_2(q, q_norm_g[l]), tabs)
        k = apply_axial_rope(rmsnorm_2(k, k_norm_g[l]), tabs)
        attn = bidirectional_gqa(q, k, v)

        xc = centred_dwconv(xr, conv_w[l], conv_b[l])
        rnn = (rg_lru(xc, rg_wa[l, 0], rg_ba[l, 0], rg_wx[l, 0], rg_bx[l, 0], rg_lambda[l, 0], False)
               + rg_lru(xc, rg_wa[l, 1], rg_ba[l, 1], rg_wx[l, 1], rg_bx[l, 1], rg_lambda[l, 1], True))
        rnn = rnn.astype(x.dtype) * jax.nn.gelu(gr)

        gates = jax.nn.sigmoid(g_merge)
        g_attn, g_rnn = gates[..., :D_MODEL], gates[..., D_MODEL:]
        mix = g_attn * attn + g_rnn * rnn
        h = h + mix @ w_out[l]

        hn = rmsnorm_2(h, norm2_g[l])
        gu = hn @ w_ffn_in[l]
        g, u = gu[..., :D_FF_2], gu[..., D_FF_2:]
        h = h + (jax.nn.silu(g) * u) @ w_ffn_out[l]

    return h[:, N_META:]


def setup_inputs(seed=0):
    out = dict(first_inputs(seed))
    for name, value in second_inputs(seed + 1).items():
        if name != "x":
            out[name + "_2"] = value
    return out


def reference(
    x, c, ctx, c_ctx, w_mod, b_mod, norm1_w, norm2_w, w_in, conv_w, conv_b, dt_bias, a_log,
    d_skip, ssd_norm_w, w_ssd_out, w_four_out, w_o, w_router, b_router, w_gate_up, b_gate_up,
    w_down, b_down, final_norm_w, meta_tokens_2, norm1_g_2, w_in_2, conv_w_2, conv_b_2, rg_wa_2,
    rg_ba_2, rg_wx_2, rg_bx_2, rg_lambda_2, q_norm_g_2, k_norm_g_2, w_out_2, norm2_g_2,
    w_ffn_in_2, w_ffn_out_2,
):
    x = first_block(
        x, c, ctx, c_ctx, w_mod, b_mod, norm1_w, norm2_w, w_in, conv_w, conv_b, dt_bias, a_log,
        d_skip, ssd_norm_w, w_ssd_out, w_four_out, w_o, w_router, b_router, w_gate_up,
        b_gate_up, w_down, b_down, final_norm_w,
    )
    return second_block(
        x, meta_tokens_2, norm1_g_2, w_in_2, conv_w_2, conv_b_2, rg_wa_2, rg_ba_2, rg_wx_2,
        rg_bx_2, rg_lambda_2, q_norm_g_2, k_norm_g_2, w_out_2, norm2_g_2, w_ffn_in_2,
        w_ffn_out_2,
    )


_drawn_inputs = setup_inputs


def setup_inputs(seed=0):
    import zlib

    import numpy as np

    out = dict(_drawn_inputs(seed))
    spreads = {}
    factors = {'ctx': 5.036,
     'c_ctx': 4.477,
     'conv_b': 4.371,
     'd_skip': 3.575,
     'ssd_norm_w': 3.002,
     'b_router': 3.294,
     'b_gate_up': 8.0,
     'b_down': 8.0,
     'rg_ba_2': 41.191,
     'rg_bx_2': 8.0,
     'q_norm_g_2': 8.0,
     'k_norm_g_2': 8.0}
    for name, (base, spread) in spreads.items():
        noise = np.random.default_rng([zlib.crc32(name.encode()), seed]).standard_normal(out[name].shape)
        drawn = base * np.exp(spread * noise) if base else spread * noise
        out[name] = __import__('jax').numpy.asarray(drawn.astype(out[name].dtype))
    for name, factor in factors.items():
        out[name] = (out[name] * factor).astype(out[name].dtype)
    return out
```

```python
from contextlib import contextmanager

import numpy as np

import concourse.bass as bass
from concourse import mybir

F32 = mybir.dt.float32
I32 = mybir.dt.int32
U32 = mybir.dt.uint32
ACT = mybir.ActivationFunctionType
ALU = mybir.AluOpType
AX = mybir.AxisListType

P = 128
D = 1024
KD = D // P
SEQ = 512
CTX = 256
TT = SEQ // P
CT = CTX // P
ALLT = TT + CT
EPS = 1e-6

N_MOD = 6
D_INNER = 2 * D
N_HEADS = 32
GROUPS = 4
HPG = N_HEADS // GROUPS
HD = 64
GW = HPG * HD
D_STATE = 128
BC_WIDTH = GROUPS * D_STATE
CONV_K = 5
FG = 8
OFF_BF = D_INNER
OFF_BB = OFF_BF + BC_WIDTH
OFF_DT = OFF_BB + BC_WIDTH
OFF_CF = OFF_DT + 2 * N_HEADS
OFF_CB = OFF_CF + BC_WIDTH
OFF_Z = OFF_CB + BC_WIDTH
OFF_F = OFF_Z + D_INNER
OFF_GF = OFF_F + D
OFF_GS = OFF_GF + D

NE = 32
TOPK = 4
BLOCKS = SEQ * TOPK // P + NE - 1
SWIGLU_LIMIT = 7.0
SWIGLU_ALPHA = 1.702

N_META = 16
T2 = SEQ + N_META
H2 = T2 // 2
NQH = 8
NKV = 2
QPK = NQH // NKV
QT = 88
NQT = T2 // QT
RNN_BLOCKS = 8
CONV_W = 4
RG_C = 8.0
D_FF2 = ((8 * D + 3 * 256 - 1) // (3 * 256)) * 256
KF = D_FF2 // P
GRID_W = 64
ROPE_THETA = 10000.0

CHUNK = KD * 4 * P


class Steps:

    def __init__(self, sem, order, rounds=1, ahead=False):
        self.sem, self.order, self.rounds = sem, list(order), rounds
        self.n = len(self.order)
        self.first = self.n if ahead else 0
        self.count = 0
        self.total = self.first + self.n * rounds
        assert len(set(self.order)) == self.n

    def open(self, eng):
        eng.sem_inc(self.sem, self.first)

    def at(self, name, it=0):
        return it * self.n + (self.first + self.order.index(name) + 1)

    def before(self, name, it):
        assert self.first
        return it * self.n + (self.order.index(name) + 1)

    def done(self, instruction, name):
        assert self.order[self.count % self.n] == name, (self.order[self.count % self.n], name)
        self.count += 1
        return instruction.then_inc(self.sem, 1)

    def after(self, eng, name, it=0):
        eng.wait_ge(self.sem, self.at(name, it))

    def after_last(self, eng, name, it):
        eng.wait_ge(self.sem, self.before(name, it))

    def all(self, eng):
        eng.wait_ge(self.sem, self.total)


class Columns:

    def __init__(self, widths):
        self.at, self.width = {}, 0
        for name, n in widths:
            self.at[name] = (self.width, n)
            self.width += n

    def __getitem__(self, name):
        a, n = self.at[name]
        return slice(a, a + n)


CST = Columns([("ident", P), ("ones", P), ("le", P), ("gt", P), ("ge", P), ("lt", P),
               ("expert", NE), ("block", BLOCKS + 1), ("eps", 1), ("one", 1)])
PRM = Columns([("c", 2 * KD), ("b_mod", 2 * N_MOD * KD), ("norm1", KD), ("norm2", KD), ("final", KD),
               ("conv", GROUPS * 8 * (CONV_K + 1)), ("ssd_norm", 2 * KD),
               ("dt_bias", 2 * N_HEADS), ("a_log", 2 * N_HEADS), ("d_skip", N_HEADS), ("b_router", NE),
               ("norm1_2", KD), ("norm2_2", KD), ("rnn", RNN_BLOCKS * 12),
               ("qk_norm", 2)])


def program(nc, io):
    FREE = (nc.sbuf_base + 31) // 32 * 32
    END = nc.sbuf_usable_end

    def at(name, shape, offset, dtype=F32):
        size = int(np.prod(shape[1:])) * 4
        assert FREE <= offset and offset + size <= END, (name, offset, size, END)
        return nc.alloc_sbuf_tensor_at(name, shape, dtype, offset=offset)

    class Area:

        def __init__(self, start, end=END):
            self.next, self.end = start, end

        def __call__(self, name, shape, dtype=F32):
            t = at(name, shape, self.next, dtype)
            self.next += (int(np.prod(shape[1:])) * 4 + 31) // 32 * 32
            assert self.next <= self.end, (name, self.next - self.end)
            return t

    area = Area(FREE)
    slot = [area(f"slot{i}", [P, CHUNK]) for i in range(6)]
    SLOT_BYTES = CHUNK * 4
    cst = area("cst", [P, CST.width])
    prm = area("prm", [P, PRM.width])
    zero = area("zero", [P, D // 4])
    STAGE = area.next
    ps = nc.alloc_psum_tensor("ps", [P, 8, 512], F32)

    ident = cst[:, CST["ident"]]
    ones = cst[:, CST["ones"]]
    eps_col = cst[:, CST["eps"]]

    def sem(name):
        return nc.alloc_semaphore(name)

    @contextmanager
    def rounds(eng, n):
        if n == 1:
            yield 0
        else:
            with eng.Fori(0, n) as it:
                yield it

    def row(w, i):
        return w[i] if isinstance(i, int) else w[bass.ds(i, 1)].rearrange("a p f -> p (a f)")

    w_loaded = [sem(f"w_loaded{i}") for i in range(6)]
    loads = [0] * 6

    class Dense:

        def __init__(self, name, w, slots, rounds, tiles, k, parts, rhs, layout, loaded=w_loaded, loads=loads):
            self.loaded = loaded
            self.w, self.slots, self.rounds, self.tiles, self.k = w, slots, rounds, tiles, k
            self.parts, self.rhs, self.layout = parts, rhs, layout
            self.n = len(slots) * tiles
            assert self.n % 2 == 0
            order = [f"tile{j}" for j in range(self.n)]
            self.pe = Steps(sem(f"{name}_summed"), order, rounds, ahead=True)
            self.ev = Steps(sem(f"{name}_taken"), order, rounds, ahead=True)
            self.first = [loads[s] for s in slots]
            for s in slots:
                loads[s] += 16 * rounds

        def width(self):
            return self.w.shape[2]

        def bank(self, j, part):
            c0, n = self.parts[part]
            return ps[:, 2 * (j % 2) + part, 0:n]

        def load(self, sp, also=None):
            self.pe.open(sp)
            with rounds(sp, self.rounds) as it:
                if also:
                    also(it)
                for i, s in enumerate(self.slots):
                    self.pe.after_last(sp, f"tile{(i + 1) * self.tiles - 1}", it)
                    src = row(self.w, it * len(self.slots) + i)
                    sp.dma_start(slot[s][:, 0:self.width()], src).then_inc(self.loaded[s], 16)

        def multiply(self, pe, after_tile=None, ready=None):
            with rounds(pe, self.rounds) as it:
                for i, s in enumerate(self.slots):
                    pe.wait_ge(self.loaded[s], it * 16 + (self.first[i] + 16))
                    for m in range(self.tiles):
                        j = i * self.tiles + m
                        if j >= 2:
                            self.ev.after(pe, f"tile{j - 2}", it)
                        else:
                            self.ev.after_last(pe, f"tile{j - 2 + self.n}", it)
                        self.tile(pe, s, m, j, ready if j == 0 else None)
                        if after_tile:
                            after_tile(j, it)

        def tile(self, pe, s, m, j, ready):
            for k in range(self.k):
                if ready:
                    ready(k)
                for part in range(len(self.parts)):
                    last = pe.matmul(self.bank(j, part), self.layout(slot[s], m, k), self.rhs(k, part),
                                     start=(k == 0), stop=(k == self.k - 1))
            self.pe.done(last, f"tile{j}")

    def k_m(k_tiles, tiles):
        def get(s, m, k):
            return s[:, (k * tiles + m) * P:(k * tiles + m + 1) * P]
        return get

    def m_k(k_tiles):
        def get(s, m, k):
            return s[:, (m * k_tiles + k) * P:(m * k_tiles + k + 1) * P]
        return get

    class Norm:

        def __init__(self, name, k, parts, src, dst, weight, bias, square, root, bank, scale_by, ready=None):
            self.ready = ready
            self.k, self.parts, self.src, self.dst = k, parts, src, dst
            self.weight, self.bias, self.square, self.root = weight, bias, square, root
            self.bank, self.scale_by = bank, scale_by
            rng = range(k)
            self.pe = Steps(sem(f"{name}_pe"), [f"sum{i}" for i in rng])
            self.act = Steps(sem(f"{name}_act"), [f"square{i}" for i in rng] + [f"root{p}" for p in range(len(parts))]
                             + ([f"bias{i}" for i in rng] if bias else []))
            self.dve = Steps(sem(f"{name}_dve"), [f"inverse{p}" for p in range(len(parts))] + [f"scaled{i}" for i in rng])

        def on_pe(self, pe):
            for i in range(self.k):
                self.act.after(pe, f"square{i}")
                for p, (c0, n) in enumerate(self.parts):
                    last = pe.matmul(ps[:, self.bank + p, 0:n], ones, self.square[i % 2][:, c0:c0 + n],
                                     start=(i == 0), stop=(i == self.k - 1))
                self.pe.done(last, f"sum{i}")

        def ready_on(self, pe):
            return lambda i: self.act.after(pe, f"bias{i}") if self.bias else self.dve.after(pe, f"scaled{i}")

        def on_act(self, act):
            for i in range(self.k):
                if i >= 2:
                    self.pe.after(act, f"sum{i - 2}")
                if self.ready:
                    self.ready(act, i)
                self.act.done(act.activation(self.square[i % 2][:, 0:self.width()], self.src(i), ACT.Square), f"square{i}")
            self.pe.after(act, f"sum{self.k - 1}")
            for p, (c0, n) in enumerate(self.parts):
                self.act.done(act.activation(self.root[:, c0:c0 + n], ps[:, self.bank + p, 0:n], ACT.Sqrt,
                                             scale=self.scale_by, bias=eps_col), f"root{p}")
            if self.bias:
                for i in range(self.k):
                    self.dve.after(act, f"scaled{i}")
                    for p, (c0, n) in enumerate(self.parts):
                        last = act.activation(self.dst(i)[:, c0:c0 + n], self.dst(i)[:, c0:c0 + n], ACT.Identity,
                                              bias=self.bias(i, p))
                    self.act.done(last, f"bias{i}")

        def on_dve(self, dve):
            self.invert(dve)
            self.scale(dve)

        def invert(self, dve):
            for p, (c0, n) in enumerate(self.parts):
                self.act.after(dve, f"root{p}")
                self.dve.done(dve.reciprocal(self.root[:, c0:c0 + n], self.root[:, c0:c0 + n]), f"inverse{p}")

        def scale(self, dve):
            self.dve.after(dve, f"inverse{len(self.parts) - 1}")
            for i in range(self.k):
                for p, (c0, n) in enumerate(self.parts):
                    last = dve.scalar_tensor_tensor(out=self.dst(i)[:, c0:c0 + n], in0=self.src(i)[:, c0:c0 + n],
                                                    scalar=self.weight(i, p), in1=self.root[:, c0:c0 + n],
                                                    op0=ALU.mult, op1=ALU.mult)
                self.dve.done(last, f"scaled{i}")

        def width(self):
            return sum(n for _, n in self.parts)

    X_PARTS = [(0, SEQ), (SEQ, CTX)]
    W1 = SEQ + CTX

    area = Area(STAGE)
    hT = area("hT", [P, KD, W1])
    mod = area("mod", [P, N_MOD * KD, 2])
    mod_scale = area("mod_scale", [P, KD, 2])
    AFTER_H = area.next
    xcT = area("xcT", [P, KD, W1])
    silu_c = area("silu_c", [P, KD, 2])
    square = [area(f"square{i}", [P, W1]) for i in range(2)]
    root = area("root", [P, W1])
    mod_row = area("mod_row", [2, 2 * D // 512, 512])
    w_dt = area("w_dt", [P, KD, 2 * N_HEADS])

    s_cst = sem("s_cst")
    s_prm = sem("s_prm")
    s_x = sem("s_x")
    c_silu = Steps(sem("c_silu"), ["silu"])
    MOD_CHUNKS = 2 * D // 512
    MOD_FIRST = 2 * KD
    mods_pe = Steps(sem("mods_pe"), [f"rows{c}" for c in range(MOD_CHUNKS)] + ["turned"])
    mods_dve = Steps(sem("mods_dve"), ["rows", "bias"])
    for c in range(MOD_CHUNKS):
        loads[c] += 16

    scale1 = Steps(sem("scale1"), ["plus1", "times"])
    norm1 = Norm("norm1", KD, X_PARTS, lambda i: xcT[:, i, :], lambda i: hT[:, i, :],
                 lambda i, p: mod_scale[:, i, p:p + 1], lambda i, p: mod[:, i, p:p + 1],
                 square, root, 4, 1.0 / D)

    DT, DT_END, OVER, INTO, DA = range(5)
    area = Area(AFTER_H)
    small = area("small", [P, 5, ALLT, 2 * N_HEADS])
    AFTER_SMALL = area.next
    area = Area(AFTER_SMALL)
    dt_raw = area("dt_raw", [P, ALLT, 2 * N_HEADS])
    soft = area("soft", [P, ALLT, 2 * N_HEADS])
    exp_a = area("exp_a", [P, 2 * N_HEADS])
    s_wdt = sem("s_wdt")
    dt_pe = Steps(sem("dt_pe"), ["raw", "end", "into", "over"])
    dt_act = Steps(sem("dt_act"), ["exp_a", "abs", "exp", "ln", "end", "into", "over"])
    dt_dve = Steps(sem("dt_dve"), ["raw", "dt", "da", "end"])
    dt_psum = ps[:, 0, 0:ALLT * 64].rearrange("p (t h) -> p t h", h=64)
    end_psum = ps[:, 1, 0:ALLT * 64].rearrange("p (t h) -> p t h", h=64)
    into_psum = ps[:, 2, 0:ALLT * 64].rearrange("p (t h) -> p t h", h=64)
    over_psum = ps[:, 3, 0:ALLT * 64].rearrange("p (t h) -> p t h", h=64)

    BLOCKS_IN = BLOCKS + 1
    expert_rows = nc.dram_tensor("expert_rows", [BLOCKS_IN * P, D], F32).ap()
    s_zero = sem("s_zero")
    s_cleared = sem("s_cleared")

    area = Area(FREE + 2 * SLOT_BYTES, FREE + 6 * SLOT_BYTES)
    x_tok = area("x_tok", [P, ALLT, GW])
    x_dt = area("x_dt", [P, TT, GW])
    x_end = area("x_end", [P, ALLT, GW])
    state = area("state", [P, TT, GW])
    y_tok = area("y_tok", [P, TT, GW])
    decay = [area(f"decay{i}", [P, HPG, P]) for i in range(2)]
    da_upto = area("da_upto", [P, HPG, P])
    y_part = area("y_part", [P, GW])
    cb_masked = [area(f"cb_masked{i}", [P, P]) for i in range(2)]
    area = Area(AFTER_SMALL)
    gate_yT = area("gate_yT", [P, 2 * KD, SEQ])
    AFTER_Y = area.next
    g_small = area("g_small", [P, 5, ALLT, 2, HPG])
    g_conv = area("g_conv", [P, 8, CONV_K + 1])
    g_skip = area("g_skip", [P, HPG])
    bT = area("bT", [P, 2, W1])
    cT = area("cT", [P, 2, SEQ])
    xT_new = [area(f"xT_new{i}", [P, W1]) for i in range(2)]
    b_tok = area("b_tok", [P, ALLT, 2, P])
    conv = area("conv", [P, W1])
    zT = area("zT", [P, 4, SEQ])

    CHUNKS = [(d, i, i if d == 0 else TT - 1 - i) for d in range(2) for i in range(TT)]
    STATES = [[TT, TT + 1, 0, 1, 2], [TT + 1, TT, 3, 2, 1]]
    TAPS = [0, 1, 3, 4]
    ssd_pe = Steps(sem("ssd_pe"),
                   ["conv0"] + [n for m in range(6) for n in (f"conv{m + 1}", f"turned{m}")] + ["conv7"]
                   + [f"state0_{i}" for i in range(5)] + ["segment0", "cb0"]
                   + [n for j in range(8) for n in
                      (([f"state1_{i}" for i in range(5)] if j == 4 else [])
                       + ([f"segment{j + 1}", f"cb{j + 1}"] if j < 7 else [])
                       + ([f"z{j // 2}"] if j % 2 else []) + [f"diagonal{j}", f"carried{j}"])]
                   + [f"yT{m}" for m in range(4)], GROUPS, ahead=True)
    ssd_act = Steps(sem("ssd_act"),
                    [n for m in range(8) for n in ([f"centre{m}", f"silu{m}"] + ([f"token{m - 1}"] if 1 <= m < 7 else []))]
                    + ["decay0"] + [n for j in range(8) for n in
                                    (([f"decay{j + 1}"] if j < 7 else []) + ([f"z{j // 2}"] if j % 2 else []))]
                    + ["z_silu"], GROUPS, ahead=True)

    def state_steps(d):
        return [f"state{d}_0", f"state{d}_1"] + [n for i in range(2, 5) for n in (f"faded{d}_{i}", f"state{d}_{i}")]

    ssd_dve = Steps(sem("ssd_dve"),
                    ["g_small", "g_conv", "g_skip"] + [f"tap{m}_{k}" for m in range(8) for k in TAPS]
                    + state_steps(0) + ["cb0", "masked0"]
                    + [n for j in range(8) for n in
                       ((state_steps(1) if j == 4 else []) + ([f"cb{j + 1}", f"masked{j + 1}"] if j < 7 else [])
                        + [f"carried{j}", f"both{j}", f"y{j}"])]
                    + [f"gated{m}" for m in range(4)], GROUPS, ahead=True)
    ssd_pool = Steps(sem("ssd_pool"),
                     ["x_end0", "x_dt0", "upto0", "skip", "upto1", "x_end1", "upto2", "upto3", "upto4", "x_dt1",
                      "upto5", "upto6", "upto7"], GROUPS, ahead=True)
    ssd_first = [loads[0], loads[1]]
    loads[0] += 16 * GROUPS
    loads[1] += 32 * GROUPS
    CONV_DST = xT_new * 2 + [bT[:, 0, :], bT[:, 1, :], cT[:, 0, :], cT[:, 1, :]]

    def conv_parts(m):
        return X_PARTS if m < 6 else X_PARTS[:1]

    def by_head(ap):
        return ap.rearrange("p (h c) -> p h c", c=HD)

    def per_head(kind, tiles, d, width=HD):
        v = g_small[:, kind, tiles, d, :]
        return v.unsqueeze(len(v.shape)).broadcast_to([*v.shape, width])

    area = Area(AFTER_Y)
    y_ssdT = area("y_ssdT", [P, KD, SEQ])
    fT = area("fT", [P, KD, SEQ])
    square_y = [area(f"square_y{i}", [P, SEQ]) for i in range(2)]
    root_y = area("root_y", [P, SEQ])
    area = Area(AFTER_Y + 2 * KD * SEQ * 4)
    c_row = area("c_row", [P, D])
    w_modT = area("w_modT", [P, D])
    mod_sum = at("mod_sum", [P, 1], AFTER_SMALL - 32)
    LATE = N_MOD * KD - MOD_FIRST
    late_dve = Steps(sem("late_dve"), ["product", "sum", "bias"], LATE, ahead=True)
    s_c_row = sem("s_c_row")
    s_modT = sem("s_modT")
    s_tile_free = sem("s_tile_free")
    c_row_silu = Steps(sem("c_row_silu"), ["silu"])
    area = Area(AFTER_SMALL)
    f_dim = area("f_dim", [P, TT, FG, 2 * P])
    area = Area(AFTER_SMALL)
    mixT = area("mixT", [P, KD, SEQ])
    x1T = area("x1T", [P, KD, SEQ])
    AFTER_X1 = area.next
    area = Area(AFTER_H)
    dft_dim = area("dft_dim", [P, 2 * P])
    gate_sT = [area(f"gate_sT{i}", [P, SEQ]) for i in range(2)]
    assert area.next <= AFTER_SMALL
    area = Area(FREE + 4 * SLOT_BYTES)
    dft_seq = area("dft_seq", [P, TT, 2, SEQ])
    f2T = area("f2T", [P, KD, SEQ])
    gate_fT = at("gate_fT", [P, KD, SEQ], AFTER_Y + KD * SEQ * 4)

    norm_y = Norm("norm_y", 2 * KD, [(0, SEQ)], lambda i: gate_yT[:, i, :], lambda i: gate_yT[:, i, :],
                  lambda i, p: prm[:, PRM["ssd_norm"].start + i:PRM["ssd_norm"].start + i + 1], None,
                  square_y, root_y, 4, 1.0 / D_INNER)
    ONE = [(0, SEQ)]
    ssd_out = Dense("ssd_out", io["w_ssd"], [0, 1, 4, 5], 1, 2, 2 * KD, ONE, lambda k, p: gate_yT[:, k, :], m_k(2 * KD))
    f_in = Dense("f_in", io["w_f"], [2, 3], 1, 4, KD, ONE, lambda k, p: hT[:, k, 0:SEQ], k_m(KD, 4))
    gate_f = Dense("gate_f", io["w_gf"], [0, 1], 1, 4, KD, ONE, lambda k, p: hT[:, k, 0:SEQ], k_m(KD, 4))
    four_out = Dense("four_out", io["w_four"], [2, 3], 1, 4, KD, ONE, lambda k, p: f2T[:, k, :], k_m(KD, 4))
    gate_s = Dense("gate_s", io["w_gs"], [0, 1], 1, 4, KD, ONE, lambda k, p: hT[:, k, 0:SEQ], k_m(KD, 4))
    w_o = Dense("w_o", io["w_o"], [2, 3], 1, 4, KD, ONE, lambda k, p: mixT[:, k, :], k_m(KD, 4))
    s_dft_dim = sem("s_dft_dim")
    s_dft_seq = sem("s_dft_seq")
    s_x1 = sem("s_x1")
    dft_pe = Steps(sem("dft_pe"), [f"dim{i}" for i in range(TT * 4)] + [f"seq{i}" for i in range(FG)])
    dft_act = Steps(sem("dft_act"), [f"dim{i}" for i in range(TT * 4)] + [f"seq{i}" for i in range(FG)])
    gate_s_act = Steps(sem("gate_s_act"), [f"sigmoid{i}" for i in range(KD)])
    mix_dve = Steps(sem("mix_dve"), [f"gated{i}" for i in range(KD)])

    area = Area(STAGE, AFTER_H)
    h2T = area("h2T", [P, KD, SEQ])
    scale2 = area("scale2", [P, KD])
    w_r = area("w_r", [P, KD, NE])
    top_w = area("top_w", [P, TT, TOPK])
    weight = area("weight", [P, TT, NE])
    row_u = area("row_u", [P, TT * TOPK], U32)
    expert_of = area("expert_of", [P, BLOCKS_IN], I32)
    n_blocks = area("n_blocks", [P, 1], I32)
    area = Area(AFTER_H, AFTER_SMALL + KD * SEQ * 4)
    logits = area("logits", [P, TT, NE])
    top = area("top", [P, TT, 8])
    top_i = area("top_i", [P, TT, 8], U32)
    top_e = area("top_e", [P, TT, TOPK])
    top_f = area("top_f", [P, TT, TOPK])
    top_sum = area("top_sum", [P, TT])
    picked = area("picked", [P, TT, TOPK, NE])
    picked2 = area("picked2", [P, TT, TOPK, NE])
    assigned = area("assigned", [P, TT, NE])
    n_of = area("n_of", [P, NE])
    end_of = area("end_of", [P, NE])
    start_of = area("start_of", [P, NE])
    row_of = area("row_of", [P, TT, NE])
    row_f = area("row_f", [P, TT * TOPK])
    ended = area("ended", [P, BLOCKS_IN, NE])
    expert_f = area("expert_f", [P, BLOCKS_IN])
    area = Area(AFTER_X1)
    h2_tok = area("h2_tok", [P, TT, D])
    square_2 = [area(f"square_2{i}", [P, SEQ]) for i in range(2)]
    root_2 = area("root_2", [P, SEQ])

    scale2_dve = Steps(sem("scale2_dve"), ["plus1", "times"])
    norm2 = Norm("norm2", KD, ONE, lambda i: x1T[:, i, :], lambda i: h2T[:, i, :],
                 lambda i, p: scale2[:, i:i + 1], lambda i, p: mod[:, 3 * KD + i, 0:1], square_2, root_2, 4, 1.0 / D)
    s_wr = sem("s_wr")
    route_pe = Steps(sem("route_pe"), ["logits"] + [f"turned{i}" for i in range(TT)] + ["ranks"]
                     + [f"turned{i}" for i in range(TT, 2 * TT)])
    route_act = Steps(sem("route_act"), [f"turned{i}" for i in range(2 * TT)] + ["exp"])
    route_dve = Steps(sem("route_dve"), ["logits"] + [f"top{t}" for t in range(TT)] + [f"index{t}" for t in range(TT)]
                      + ["minus_max", "expert", "picked", "assigned",
                         "n0", "n1", "n2", "n3", "end", "start", "row_of", "picked_row", "row", "row_u",
                         "ended", "expert_f", "expert_of", "n_blocks", "sum", "inverse", "top_w", "picked_w", "weight"])
    s_placed = sem("s_placed")

    area = Area(AFTER_H, AFTER_SMALL + KD * SEQ * 4)
    x_row = area("x_row", [P, D])
    xT_blk = area("xT_blk", [P, KD, P])
    y_row = area("y_row", [P, D])
    b_row = area("b_row", [P, 2, D])
    area = Area(AFTER_X1)
    gate = [area(f"gate{j}", [P, 512]) for j in range(2)]
    up = [area(f"up{j}", [P, 512]) for j in range(2)]
    sig = [area(f"sig{j}", [P, 512]) for j in range(2)]
    aT = area("aT", [P, KD, P])
    exp_first = list(loads)
    moe_pe = Steps(sem("moe_pe"), ["gate0", "up0", "gate1", "aT0", "up1", "xT", "aT1", "down0", "down1"], 1, ahead=True)
    moe_act = Steps(sem("moe_act"), ["sigmoid0", "aT0", "sigmoid1", "xT", "aT1", "y"], 1, ahead=True)
    moe_dve = Steps(sem("moe_dve"), [f"{n}{j}" for j in range(2) for n in ("gate", "up", "gate_min", "up_clip", "times", "act")],
                    1, ahead=True)
    s_xrow = sem("s_xrow")
    s_brow = sem("s_brow")
    s_yrow = sem("s_yrow")
    s_all_stored = sem("s_all_stored")
    x0_pe = Steps(sem("x0_pe"), ["xT"])
    x0_act = Steps(sem("x0_act"), ["xT"])

    def block_rows(t, i):
        return t[bass.ds(i * P, P), :]

    area = Area(FREE + 3 * SLOT_BYTES, FREE + 6 * SLOT_BYTES)
    picked_rows = [area(f"picked_rows{i}", [P, TOPK, D]) for i in range(2)]
    moe_tok = [area(f"moe_tok{i}", [P, D]) for i in range(2)]
    area = Area(AFTER_X1)
    b_dn = area("b_dn", [NE, D])
    weightT = area("weightT", [NE, TT, P])
    square_f = [area(f"square_f{i}", [P, SEQ]) for i in range(2)]
    root_f = area("root_f", [P, SEQ])
    AFTER_FINAL = area.next
    s_bdn = sem("s_bdn")
    s_rows = [sem("s_rows0"), sem("s_rows1")]
    back_pe = Steps(sem("back_pe"), ["weightT"] + [n for t in range(TT) for n in (f"bias{t}", f"turned{t}")])
    back_act = Steps(sem("back_act"), ["weightT"])
    back_dve = Steps(sem("back_dve"), [n for t in range(TT) for n in (*[f"add{t}_{k}" for k in range(TOPK)], f"bias{t}",
                                                                     *([f"x2{t - 1}"] if t else []))] + [f"x2{TT - 1}"])

    H_PARTS = [(0, H2), (H2, H2)]
    area = Area(STAGE)
    h2nd = area("h2nd", [P, KD, T2])
    xnT = area("xnT", [P, KD, T2])
    assert area.next <= AFTER_X1 - KD * SEQ * 4
    attnT = area("attnT", [P, KD + 1, T2])
    kT = area("kT", [P, NKV, T2])
    v_tok = area("v_tok", [QT, NKV, NQT, P])
    rnn_prm = area("rnn_prm", [P, RNN_BLOCKS, 12])
    AFTER_V = max(area.next, AFTER_X1)
    attn_flat = attnT[:].rearrange("p k t -> p (k t)")

    w2_loaded = [sem(f"w2_loaded{i}") for i in range(6)]
    loads2 = [0] * 6
    second = dict(loaded=w2_loaded, loads=loads2)

    final = Norm("final", KD, ONE, lambda i: x1T[:, i, :], lambda i: h2nd[:, i, N_META:T2],
                 lambda i, p: prm[:, PRM["final"].start + i:PRM["final"].start + i + 1], None, square_f, root_f, 4, 1.0 / D)
    area = Area(AFTER_FINAL)
    square_n = [area(f"square_n{i}", [P, T2]) for i in range(2)]
    root_n = area("root_n", [P, T2])
    AFTER_ROOT_N = area.next
    s_meta = sem("s_meta")

    def final_ready(act, i):
        final.dve.after(act, f"scaled{i}")

    norm1_2 = Norm("norm1_2", KD, H_PARTS, lambda i: h2nd[:, i, :], lambda i: xnT[:, i, :],
                   lambda i, p: prm[:, PRM["norm1_2"].start + i:PRM["norm1_2"].start + i + 1], None,
                   square_n, root_n, 6, 1.0 / D, ready=final_ready)

    area = Area(AFTER_V)
    rope = area("rope", [P, 2 * T2 + P])
    square_h = [area(f"square_h{i}", [P, 2, H2]) for i in range(2)]
    raw_h = [area(f"raw_h{i}", [P, 2, H2]) for i in range(2)]
    root_h = [area(f"root_h{i}", [P, 2, H2]) for i in range(2)]
    cos_h = [area(f"cos_h{i}", [P, 2, H2]) for i in range(2)]
    sin_h = area("sin_h", [P, 2, H2])
    vT = [area(f"vT{i}", [P, 2, H2]) for i in range(2)]
    cos_table = rope[:, 0:T2].rearrange("p (a c) -> p a c", a=2)
    sin_table = rope[:, T2:2 * T2].rearrange("p (a c) -> p a c", a=2)
    turn = rope[:, 2 * T2:]
    s_rope = sem("s_rope")

    q_in = Dense("q_in", io["w_q"], [0, 1], 2, 2, KD, H_PARTS, lambda k, p: xnT[:, k, p * H2:(p + 1) * H2], k_m(KD, 2), **second)
    kv_in = Dense("kv_in", io["w_kv"], [2], 1, 4, KD, H_PARTS, lambda k, p: xnT[:, k, p * H2:(p + 1) * H2], k_m(KD, 4), **second)

    class Rotary:

        def __init__(self, name, dense, n, weight, dst):
            self.dense, self.n, self.weight, self.dst = dense, n, weight, dst
            rng = range(n)
            self.pe = Steps(sem(f"{name}_pe"), [s for j in rng for s in (f"sum{j}", f"turn{j}")], dense.rounds, ahead=True)
            self.act = Steps(sem(f"{name}_act"), [s for j in rng for s in (f"square{j}", f"root{j}")], dense.rounds, ahead=True)
            self.dve = Steps(sem(f"{name}_dve"), [f"{s}{j}" for j in rng for s in ("cos", "inverse", "sin", "add", "out")],
                             dense.rounds, ahead=True)

        def wait(self, steps, eng, name, j, it):
            if j >= 0:
                steps.after(eng, f"{name}{j}", it)
            else:
                steps.after_last(eng, f"{name}{j + self.n}", it)

        def on_pe(self, pe, j, it):
            self.dense.ev.after(pe, f"tile{j}", it)
            self.wait(self.act, pe, "root", j - 1, it)
            for p in range(2):
                last = pe.matmul(ps[:, 4 + p, 0:H2], ones, square_h[j % 2][:, p], start=True, stop=True)
            self.pe.done(last, f"sum{j}")
            self.wait(self.dve, pe, "sin", j - 1, it)
            for p in range(2):
                last = pe.matmul(ps[:, 6 + p, 0:H2], turn, raw_h[j % 2][:, p], start=True, stop=True)
            self.pe.done(last, f"turn{j}")

        def on_act(self, act, j, it):
            src = ps[:, 2 * (j % 2):2 * (j % 2) + 2, 0:H2]
            self.dense.pe.after(act, f"tile{j}", it)
            self.wait(self.pe, act, "turn", j - 2, it)
            self.act.done(act.activation(square_h[j % 2][:], src, ACT.Square), f"square{j}")
            self.wait(self.dve, act, "out", j - 2, it)
            self.dense.ev.done(act.activation(raw_h[j % 2][:], src, ACT.Copy, scale=self.weight), f"tile{j}")
            self.pe.after(act, f"sum{j}", it)
            self.act.done(act.activation(root_h[j % 2][:], ps[:, 4:6, 0:H2], ACT.Sqrt, scale=1.0 / P, bias=eps_col), f"root{j}")

        def on_dve(self, dve, j, it):
            self.dense.ev.after(dve, f"tile{j}", it)
            self.wait(self.dve, dve, "out", j - 1, it)
            self.dve.done(dve.tensor_tensor(cos_h[j % 2][:], raw_h[j % 2][:], cos_table, ALU.mult), f"cos{j}")
            self.act.after(dve, f"root{j}", it)
            self.dve.done(dve.reciprocal(root_h[j % 2][:], root_h[j % 2][:]), f"inverse{j}")
            self.pe.after(dve, f"turn{j}", it)
            self.dve.done(dve.tensor_tensor(sin_h[:], ps[:, 6:8, 0:H2], sin_table, ALU.mult), f"sin{j}")
            self.dve.after(dve, f"sin{j}", it)
            self.dve.done(dve.tensor_tensor(cos_h[j % 2][:], cos_h[j % 2][:], sin_h[:], ALU.add), f"add{j}")
            self.dve.after(dve, f"add{j}", it)
            self.dve.done(dve.tensor_tensor(self.dst(it, j), cos_h[j % 2][:], root_h[j % 2][:], ALU.mult), f"out{j}")

    q_rot = Rotary("q_rot", q_in, 4, prm[:, PRM["qk_norm"].start:PRM["qk_norm"].start + 1],
                   lambda it, j: attn_flat[:, bass.ds(it * (4 * T2) + j * T2, T2)].rearrange("p (a c) -> p a c", a=2))
    k_rot = Rotary("k_rot", kv_in, NKV, prm[:, PRM["qk_norm"].start + 1:PRM["qk_norm"].start + 2],
                   lambda it, j: kT[:, j, :].rearrange("p (a c) -> p a c", a=2))
    v_pe = Steps(sem("v_pe"), ["turned0", "turned1"])
    v_act = Steps(sem("v_act"), ["tok0", "tok1"])
    lam_act = Steps(sem("lam_act"), ["abs", "exp", "ln"])
    lam_dve = Steps(sem("lam_dve"), ["copy", "min", "times"])
    lam = rnn_prm[:, :, 10:12]
    lam_abs = at("lam_abs", [P, RNN_BLOCKS, 2], AFTER_ROOT_N)

    area = Area(AFTER_V)
    q_now = area("q_now", [P, T2])
    probs = [area(f"probs{i}", [QT, 2, H2]) for i in range(2)]
    probsT = area("probsT", [QT, NQT, T2])
    inverse_of = [area(f"inverse_of{i}", [QT, QT]) for i in range(2)]
    row_max = area("row_max", [QT, NQT])
    row_sum = area("row_sum", [QT, NQT])
    HEAD_SCALE = P ** -0.5
    NT = range(NQT)
    LAG = 2
    attn_pe = Steps(sem("attn_pe"), [s for t in range(1, NQT) for s in (f"scores{t}", *([f"turned{t - LAG}"] if t >= LAG else []))]
                    + ["scores_next"] + [f"turned{t}" for t in range(NQT - LAG, NQT)] + ["out"], NQH, ahead=True)
    attn_act = Steps(sem("attn_act"), [f"exp{t}" for t in NT], NQH, ahead=True)
    attn_dve = Steps(sem("attn_dve"), ["sum0", "inverse0"]
                     + [s for t in range(1, NQT) for s in (*(["q_next"] if t == NQT - 1 else []), f"max{t}", f"minus{t}",
                                                           *([f"turned{t - LAG}"] if t >= LAG else []), f"sum{t}", f"inverse{t}")]
                     + [f"turned{t}" for t in range(NQT - LAG, NQT)] + ["max_next", "minus_next", "out"], NQH, ahead=True)
    first_pe = Steps(sem("first_pe"), ["scores"], NKV)
    first_dve = Steps(sem("first_dve"), ["q"] + [f"{s}{kv}" for kv in range(NKV) for s in ("max", "minus")])
    s_ninth = sem("s_ninth")

    area = Area(AFTER_V)
    x_pad = area("x_pad", [P, T2 + CONV_W - 1])
    xcv = area("xcv", [P, T2])
    gr = area("gr", [P, T2])
    gelu_in = area("gelu_in", [P, T2])
    r_gate = [area(f"r_gate{d}", [P, T2]) for d in range(2)]
    i_gate = [area(f"i_gate{d}", [P, T2]) for d in range(2)]
    rg_decay = [area(f"rg_decay{d}", [P, T2]) for d in range(2)]
    hidden = [area(f"hidden{d}", [P, T2]) for d in range(2)]
    merge_attn = area("merge_attn", [P, T2])
    merge_rnn = area("merge_rnn", [P, T2])
    one_prm = area("one_prm", [P, 12])
    GELU_CUBE, GELU_SCALE = 0.044715, 2 * (2 / np.pi) ** 0.5

    def halves(t):
        return t.rearrange("p (a c) -> p a c", a=2)

    rnn_in = Dense("rnn_in", io["w_rnn"], [3, 4], RNN_BLOCKS, 2, KD, H_PARTS, lambda k, p: xnT[:, k, p * H2:(p + 1) * H2],
                   k_m(KD, 2), **second)
    s_rg = sem("s_rg")
    rg_pe = Steps(sem("rg_pe"), ["gates0", "gates1"], RNN_BLOCKS, ahead=True)
    rg_act = Steps(sem("rg_act"), ["gelu", "r0", "i0", "r1", "i1", "exp0", "tanh0", "exp1", "tanh1", "sqrt0", "sqrt1"], RNN_BLOCKS, ahead=True)
    rg_dve = Steps(sem("rg_dve"), ["params"] + [f"conv{j}" for j in range(CONV_W)] + ["gelu_square", "cube", "gelu_in", "gelu", "ix0", "attn", "ix1"]
                   + ["ratio0", "ratio1", "input0", "scan0", "input1", "scan1",
                      "both", "merged", "out"], RNN_BLOCKS, ahead=True)
    rg_pool = Steps(sem("rg_pool"), ["square0", "square1", "gelued"], RNN_BLOCKS)
    s_pad = sem("s_pad")

    area = Area(AFTER_V)
    square_m = [area(f"square_m{i}", [P, T2]) for i in range(2)]
    root_m = area("root_m", [P, T2])
    area = Area(STAGE + 2 * KD * T2 * 4)
    ffn_act = area("ffn_act", [P, KF, T2])
    ffn_gate = [area(f"ffn_gate{i}", [P, T2]) for i in range(2)]
    y_out = [area(f"y_out{i}", [P, T2]) for i in range(2)]
    ffn_flat = ffn_act[:].rearrange("p k t -> p (k t)")
    h2nd_flat = h2nd[:].rearrange("p k t -> p (k t)")

    out2 = Dense("out2", io["w_out2"], [0, 1], 1, 4, KD, H_PARTS, lambda k, p: attnT[:, k, p * H2:(p + 1) * H2], k_m(KD, 4), **second)
    norm2_2 = Norm("norm2_2", KD, H_PARTS, lambda i: h2nd[:, i, :], lambda i: xnT[:, i, :],
                   lambda i, p: prm[:, PRM["norm2_2"].start + i:PRM["norm2_2"].start + i + 1], None,
                   square_m, root_m, 4, 1.0 / D, ready=lambda act, i: out2.ev.after(act, f"tile{i}"))
    ffn_in = Dense("ffn_in", io["w_ffn"], [2, 3], KF // 2, 2, KD, H_PARTS, lambda k, p: xnT[:, k, p * H2:(p + 1) * H2],
                   k_m(KD, 2), **second)
    ffn_out = Dense("ffn_out", io["w_ffn_out"], [4, 5], KD // 2, 1, KF, H_PARTS, lambda k, p: ffn_act[:, k, p * H2:(p + 1) * H2],
                    m_k(KF), **second)
    ffn_sig = Steps(sem("ffn_sig"), ["gate0", "gate1"], ffn_in.rounds, ahead=True)
    s_out = [sem(f"s_out{i}") for i in range(2)]

    block_scope = nc.Block()
    block = block_scope.__enter__()

    @block.sync
    def _(sp):
        for c in range(MOD_CHUNKS):
            if c == MOD_CHUNKS // 2:
                sp.dma_start(xcT[:], io["xcT"]).then_inc(s_x, 16)
            sp.dma_start(slot[c][:], io["w_mod"][c]).then_inc(w_loaded[c], 16)

        mods_pe.after(sp, f"rows{MOD_CHUNKS - 1}")
        sp.wait_ge(s_zero, 1)
        ssd_pe.open(sp)
        with sp.Fori(0, GROUPS) as g:
            ssd_pe.after_last(sp, "conv3", g)
            sp.dma_start(slot[0][:], io["w_xbc"][bass.ds(g * 2, 1)].rearrange("a p f -> p (a f)")).then_inc(w_loaded[0], 16)
            ssd_pe.after_last(sp, "z3", g)
            sp.dma_start(slot[1][:], io["w_xbc"][bass.ds(g * 2 + 1, 1)].rearrange("a p f -> p (a f)")).then_inc(w_loaded[1], 16)
            ssd_pe.after(sp, "conv7", g)
            sp.dma_start(slot[1][:], io["w_z"][bass.ds(g, 1)].rearrange("a p f -> p (a f)")).then_inc(w_loaded[1], 16)
            quarter = expert_rows[bass.ds(g * (BLOCKS_IN * P // GROUPS), BLOCKS_IN * P // GROUPS), :]
            sp.dma_start(quarter.rearrange("(p b) (q c) -> p (b q) c", p=P, c=D // 4),
                         zero[:].unsqueeze(1).broadcast_to([P, BLOCKS_IN // GROUPS * 4, D // 4])).then_inc(s_cleared, 16)

        ssd_pe.after(sp, "z3", GROUPS - 1)
        ssd_dve.all(sp)
        ssd_out.load(sp)
        f_in.load(sp)
        ssd_out.pe.all(sp)
        sp.dma_start(dft_seq[:], io["dft_seq"]).then_inc(s_dft_seq, 16)
        gate_f.load(sp)
        f_in.pe.all(sp)
        four_out.load(sp)
        gate_f.pe.all(sp)
        gate_s.load(sp)
        four_out.pe.all(sp)
        w_o.load(sp)

        w_o.pe.all(sp)
        route_dve.after(sp, "n_blocks")
        moe_pe.open(sp)
        n = sp.value_load(n_blocks[0:1, 0:1], min_val=1, max_val=BLOCKS)
        with sp.Fori(0, n) as i:
            e = sp.value_load(expert_of[0:1, bass.ds(i, 1)], min_val=0, max_val=NE - 1)
            for c, free in enumerate(["gate0", "up0", "gate1", "up1", "down0", "down1"]):
                if c == 1:
                    moe_pe.after_last(sp, "xT", i)
                    x0_pe.all(sp)
                    sp.dma_start(x_row[:], block_rows(expert_rows, i + 1)).then_inc(s_xrow, 16)
                if c == 4:
                    moe_dve.after_last(sp, "up1", i)
                    sp.dma_start(b_row[:].rearrange("p h d -> p (h d)"),
                                 io["b_gu"][bass.ds(e, 1), :].partition_broadcast(P)).then_inc(s_brow, 16)
                moe_pe.after_last(sp, free, i)
                sp.dma_start(slot[c][:], row(io["w_exp"], e * 6 + c)).then_inc(w_loaded[c], 16)

        sp.wait_ge(moe_pe.sem, n * moe_pe.n + moe_pe.first)
        q_in.load(sp)
        kv_in.load(sp)

        back_pe.all(sp)

        def load_rg(it):
            rg_pe.after_last(sp, "gates1", it)
            sp.dma_start(slot[5][:, 0:4 * P], row(io["w_rg"], it)).then_inc(s_rg, 16)

        rnn_in.load(sp, load_rg)

        q_in.pe.all(sp)
        out2.load(sp)
        kv_in.pe.all(sp)
        rnn_in.pe.all(sp)
        ffn_in.load(sp)
        ffn_out.load(sp)

    @block.scalar
    def _(act):
        act.dma_start(prm[:], io["prm"]).then_inc(s_prm, 16)
        act.dma_start(cst[:], io["cst"]).then_inc(s_cst, 16)
        act.dma_start(w_dt[:], io["w_dt"]).then_inc(s_wdt, 16)
        act.wait_ge(s_prm, 16)
        c_silu.done(act.activation(silu_c[:].rearrange("p k c -> p (k c)"), prm[:, PRM["c"]], ACT.Silu), "silu")
        act.wait_ge(s_cst, 16)
        act.wait_ge(s_x, 16)
        norm1.on_act(act)

        norm1.dve.all(act)
        dt_act.done(act.activation(exp_a[:], prm[:, PRM["a_log"]], ACT.Exp), "exp_a")
        dt_dve.after(act, "raw")
        dt_act.done(act.activation(soft[:], dt_raw[:], ACT.Abs), "abs")
        dt_act.after(act, "abs")
        dt_act.done(act.activation(soft[:], soft[:], ACT.Exp, scale=-1.0), "exp")
        dt_act.after(act, "exp")
        dt_act.done(act.activation(soft[:], soft[:], ACT.Ln, bias=cst[:, CST["one"]]), "ln")
        dt_pe.after(act, "end")
        dt_act.done(act.activation(small[:, DT_END], end_psum, ACT.Exp), "end")
        dt_pe.after(act, "into")
        dt_act.done(act.activation(small[:, INTO], into_psum, ACT.Exp), "into")
        dt_pe.after(act, "over")
        dt_act.done(act.activation(small[:, OVER], over_psum, ACT.Exp), "over")

        ssd_act.open(act)
        with act.Fori(0, GROUPS) as g:
            for m in range(8):
                ssd_pe.after(act, f"conv{m}", g)
                if m == 0:
                    ssd_dve.after(act, "g_skip", g)
                    ssd_act.after_last(act, "z_silu", g)
                else:
                    ssd_act.after(act, f"silu{m - 1}", g)
                for part, (c0, n) in enumerate(conv_parts(m)):
                    last = act.activation(conv[:, c0:c0 + n], ps[:, 2 * (m % 2) + part, 0:n], ACT.Identity,
                                          scale=g_conv[:, m, 2:3], bias=g_conv[:, m, CONV_K:CONV_K + 1])
                ssd_act.done(last, f"centre{m}")
                ssd_dve.after(act, f"tap{m}_4", g)
                n = sum(n for _, n in conv_parts(m))
                if 2 <= m < 4:
                    ssd_pe.after(act, f"turned{m - 2}", g)
                ssd_act.done(act.activation(CONV_DST[m][:, 0:n], conv[:, 0:n], ACT.Silu), f"silu{m}")
                if 1 <= m < 7:
                    u = m - 1
                    ssd_pe.after(act, f"turned{u}", g)
                    if u == 0:
                        ssd_pool.after_last(act, "upto7", g)
                    bank = 4 + 2 * (u % 2)
                    for lo, hi in ((0, 4), (4, 6)):
                        src = ps[:, bank + lo // 4, 0:(hi - lo) * P].rearrange("p (t c) -> p t c", c=P)
                        dst = x_tok[:, lo:hi, u * P:(u + 1) * P] if u < 4 else b_tok[:, lo:hi, u - 4, :]
                        last = act.activation(dst, src, ACT.Copy)
                    ssd_act.done(last, f"token{u}")

            def decays(j):
                ssd_pe.after(act, f"segment{j}", g)
                ssd_act.done(act.activation(decay[j % 2][:].rearrange("p (q h) l -> p q (h l)", q=2), ps[:, 0:2, :],
                                            ACT.Exp), f"decay{j}")

            decays(0)
            for j in range(8):
                if j < 7:
                    decays(j + 1)
                if j % 2:
                    m = j // 2
                    ssd_pe.after(act, f"z{m}", g)
                    ssd_act.done(act.activation(zT[:, m, :], ps[:, 3, :], ACT.Copy), f"z{m}")
            ssd_act.after(act, "z3", g)
            ssd_act.done(act.activation(zT[:], zT[:], ACT.Silu), "z_silu")

        ssd_dve.all(act)
        ssd_pe.all(act)
        ssd_pool.all(act)
        norm_y.on_act(act)
        act.dma_start(dft_dim[:], io["dft_dim"]).then_inc(s_dft_dim, 16)
        for stage in (ssd_out, f_in, gate_f):
            stage.ev.open(act)
        for j in range(ssd_out.n):
            ssd_out.pe.after(act, f"tile{j}")
            ssd_out.ev.done(act.activation(y_ssdT[:, j, :], ssd_out.bank(j, 0), ACT.Copy), f"tile{j}")
            if j == 0:
                act.wait_ge(s_c_row, 16)
                c_row_silu.done(act.activation(c_row[:], c_row[:], ACT.Silu), "silu")
        for j in range(f_in.n):
            f_in.pe.after(act, f"tile{j}")
            f_in.ev.done(act.activation(fT[:, j, :], f_in.bank(j, 0), ACT.Copy), f"tile{j}")
        for i in range(TT * 4):
            dft_pe.after(act, f"dim{i}")
            dft_act.done(act.activation(f_dim[:].rearrange("p t (q g) c -> p (t q) (g c)", g=2)[:, i, :],
                                        ps[:, 4 + i % 4, :], ACT.Copy), f"dim{i}")
        for i in range(FG):
            dft_pe.after(act, f"seq{i}")
            dft_act.done(act.activation(f2T[:, i, :], ps[:, 4 + i % 4, :], ACT.Copy), f"seq{i}")
        for j in range(gate_f.n):
            gate_f.pe.after(act, f"tile{j}")
            gate_f.ev.done(act.activation(gate_fT[:, j, :], gate_f.bank(j, 0), ACT.Sigmoid), f"tile{j}")
        dft_pe.all(act)
        act.dma_start(x1T[:], io["xcT"][:, :, 0:SEQ]).then_inc(s_x1, 16)
        for j in range(gate_s.n):
            gate_s.pe.after(act, f"tile{j}")
            if j >= 2:
                mix_dve.after(act, f"gated{j - 2}")
            gate_s_act.done(act.activation(gate_sT[j % 2][:], gate_s.bank(j, 0), ACT.Sigmoid), f"sigmoid{j}")

        w_o.ev.all(act)
        act.dma_start(w_r[:], io["w_router"]).then_inc(s_wr, 16)
        norm2.on_act(act)
        for i in range(2 * TT):
            route_pe.after(act, f"turned{i}")
            route_act.done(act.activation(h2_tok[:, i // 2, (i % 2) * 512:(i % 2 + 1) * 512], ps[:, 4 + i % 4, :], ACT.Copy),
                           f"turned{i}")
        route_dve.after(act, "minus_max")
        route_act.done(act.activation(top_e[:], top_e[:], ACT.Exp), "exp")

        moe_act.open(act)
        act.sem_inc(s_yrow, 16)
        route_dve.all(act)
        act.wait_ge(s_placed, 16 * TT * TOPK)
        act.dma_start(x_row[:], expert_rows[0:P, :]).then_inc(s_xrow, 16)
        n = act.value_load(n_blocks[0:1, 0:1], min_val=1, max_val=BLOCKS)
        x0_pe.all(act)
        x0_act.done(act.activation(xT_blk[:].rearrange("p (h k) c -> p h (k c)", h=2), ps[:, 4:6, :], ACT.Copy), "xT")
        with act.Fori(0, n) as i:
            for j in range(2):
                moe_dve.after(act, f"gate_min{j}", i)
                moe_act.done(act.activation(sig[j][:], gate[j][:], ACT.Sigmoid, scale=SWIGLU_ALPHA), f"sigmoid{j}")
                if j:
                    moe_pe.after(act, "xT", i)
                    moe_act.done(act.activation(xT_blk[:].rearrange("p (h k) c -> p h (k c)", h=2), ps[:, 4:6, :], ACT.Copy), "xT")
                moe_pe.after(act, f"aT{j}", i)
                moe_act.done(act.activation(aT[:, 4 * j:4 * j + 4, :].rearrange("p k c -> p (k c)"), ps[:, j, :], ACT.Copy), f"aT{j}")
            moe_pe.after(act, "down1", i)
            act.wait_ge(s_yrow, i * 16 + 16)
            moe_act.done(act.activation(y_row[:].rearrange("p (h c) -> p h c", h=2), ps[:, 6:8, :], ACT.Copy), "y")
            moe_act.after(act, "y", i)
            act.dma_start(block_rows(expert_rows, i), y_row[:]).then_inc(s_yrow, 16)

        act.wait_ge(s_yrow, n * 16 + 16)
        act.sem_inc(s_all_stored, 1)
        act.dma_start(b_dn[:], io["b_down"]).then_inc(s_bdn, 16)
        back_pe.after(act, "weightT")
        back_act.done(act.activation(weightT[:], ps[0:NE, 4, 0:TT * P].rearrange("p (t c) -> p t c", c=P), ACT.Copy), "weightT")

        back_dve.all(act)
        act.dma_start(h2nd[:, :, 0:N_META], io["metaT"]).then_inc(s_meta, 16)
        final.on_act(act)
        act.wait_ge(s_meta, 16)
        norm1_2.on_act(act)
        act.dma_start(rope[:], io["rope"]).then_inc(s_rope, 16)
        lam_dve.after(act, "copy")
        lam_act.done(act.activation(lam_abs[:], lam, ACT.Abs), "abs")
        lam_act.after(act, "abs")
        lam_act.done(act.activation(lam_abs[:], lam_abs[:], ACT.Exp, scale=-1.0), "exp")
        lam_act.after(act, "exp")
        lam_act.done(act.activation(lam_abs[:], lam_abs[:], ACT.Ln, bias=cst[:, CST["one"]]), "ln")
        q_in.ev.open(act)
        q_rot.act.open(act)
        with rounds(act, q_in.rounds) as it:
            for j in range(q_in.n):
                q_rot.on_act(act, j, it)
        kv_in.ev.open(act)
        k_rot.act.open(act)
        q_rot.dve.all(act)
        for j in range(NKV):
            k_rot.on_act(act, j, 0)
        for j in range(NKV):
            kv_in.pe.after(act, f"tile{NKV + j}")
            kv_in.ev.done(act.activation(vT[j][:], ps[:, 2 * j:2 * j + 2, 0:H2], ACT.Copy), f"tile{NKV + j}")
        for j in range(NKV):
            v_pe.after(act, f"turned{j}")
            v_act.done(act.activation(v_tok[:, j].rearrange("p (a t) c -> p a (t c)", a=2), ps[0:QT, 4 + 2 * j:6 + 2 * j, 0:3 * P],
                                      ACT.Copy), f"tok{j}")

        attn_act.open(act)
        v_act.all(act)
        k_rot.dve.all(act)
        for kv in range(NKV):
            first_dve.after(act, f"minus{kv}")
            with act.Fori(0, QPK) as h:
                it = h + kv * QPK
                for t in NT:
                    if t:
                        attn_dve.after(act, f"minus{t}", it)
                    else:
                        attn_dve.after_last(act, "minus_next", it)
                    if t >= 2:
                        attn_pe.after(act, f"turned{t - 2}", it)
                    attn_act.done(act.activation(probs[t % 2][:], ps[0:QT, 2 * (t % 2):2 * (t % 2) + 2, 0:H2], ACT.Exp,
                                                 scale=HEAD_SCALE, bias=row_max[:, t:t + 1], accum_out=row_sum[:, t:t + 1]), f"exp{t}")

        rnn_in.ev.open(act)
        rg_act.open(act)
        attn_dve.all(act)
        lam_dve.all(act)
        with rounds(act, RNN_BLOCKS) as it:
            rnn_in.pe.after(act, "tile0", it)
            rg_dve.after_last(act, f"conv{CONV_W - 1}", it)
            rnn_in.ev.done(act.activation(halves(x_pad[:, CONV_W // 2:CONV_W // 2 + T2]), ps[:, 0:2, 0:H2], ACT.Copy), "tile0")
            rg_dve.after_last(act, "out", it)
            rnn_in.pe.after(act, "tile1", it)
            rnn_in.ev.done(act.activation(halves(gr[:]), ps[:, 2:4, 0:H2], ACT.Copy), "tile1")
            rg_dve.after(act, "gelu_in", it)
            rg_act.done(act.activation(gelu_in[:], gelu_in[:], ACT.Sigmoid, scale=GELU_SCALE), "gelu")
            for d in range(2):
                rg_pe.after(act, f"gates{d}", it)
                rg_act.done(act.activation(halves(r_gate[d][:]), ps[:, 4:6, 0:H2], ACT.Sigmoid, bias=one_prm[:, 6 + d:7 + d]), f"r{d}")
                rg_act.done(act.activation(halves(i_gate[d][:]), ps[:, 6:8, 0:H2], ACT.Sigmoid, bias=one_prm[:, 8 + d:9 + d]), f"i{d}")
                if d == 0:
                    rnn_in.pe.after(act, "tile2", it)
                    rnn_in.ev.done(act.activation(halves(merge_attn[:]), ps[:, 0:2, 0:H2], ACT.Sigmoid), "tile2")
            for d in range(2):
                rg_act.after(act, f"r{d}", it)
                rg_act.done(act.activation(rg_decay[d][:], r_gate[d][:], ACT.Exp, scale=one_prm[:, 10 + d:11 + d]), f"exp{d}")
                rg_act.after(act, f"exp{d}", it)
                rg_act.done(act.activation(r_gate[d][:], r_gate[d][:], ACT.Tanh, scale=one_prm[:, 10 + d:11 + d]), f"tanh{d}")
            for d in range(2):
                rg_dve.after(act, f"ratio{d}", it)
                rg_act.done(act.activation(r_gate[d][:], r_gate[d][:], ACT.Sqrt, scale=-1.0), f"sqrt{d}")
            rnn_in.pe.after(act, "tile3", it)
            rnn_in.ev.done(act.activation(halves(merge_rnn[:]), ps[:, 2:4, 0:H2], ACT.Sigmoid), "tile3")

        norm2_2.on_act(act)
        ffn_sig.open(act)
        norm2_2.dve.all(act)
        with rounds(act, ffn_in.rounds) as it:
            for i in range(2):
                ffn_in.pe.after(act, f"tile{2 * i}", it)
                ffn_in.ev.after_last(act, f"tile{2 * i + 1}", it)
                ffn_sig.done(act.activation(halves(ffn_gate[i][:]), ps[:, 0:2, 0:H2], ACT.Sigmoid), f"gate{i}")
        for i in range(2):
            act.sem_inc(s_out[i], 16)
        with rounds(act, ffn_out.rounds) as it:
            for i in range(2):
                ffn_out.ev.after(act, f"tile{i}", it)
                act.dma_start(row(io["out"], it * 2 + i), y_out[i][:, N_META:T2]).then_inc(s_out[i], 16)
        for i in range(2):
            act.wait_ge(s_out[i], 16 + 16 * ffn_out.rounds)

    @block.tensor
    def _(pe):
        c_silu.all(pe)
        pe.wait_ge(s_cst, 16)
        for c in range(MOD_CHUNKS):
            if c == MOD_CHUNKS // 2:
                norm1.on_pe(pe)
            pe.wait_ge(w_loaded[c], 16)
            for k in range(KD):
                last = pe.matmul(ps[0:2, c, :], silu_c[:, k, :], slot[c][:, k * 512:(k + 1) * 512], start=(k == 0), stop=(k == KD - 1))
            mods_pe.done(last, f"rows{c}")
        mods_dve.after(pe, "rows")
        for m in range(MOD_FIRST):
            last = pe.transpose(ps[:, 6, 2 * m:2 * m + 2], mod_row[:, m // 4, (m % 4) * P:(m % 4 + 1) * P], cst[0:2, 0:2])
        mods_pe.done(last, "turned")

        norm1_ready = norm1.ready_on(pe)
        pe.wait_ge(s_wdt, 16)
        for t in range(ALLT):
            for k in range(KD):
                if t == 0:
                    norm1_ready(k)
                last = pe.matmul(dt_psum[:, t, :], hT[:, k, t * P:(t + 1) * P], w_dt[:, k, :], start=(k == 0), stop=(k == KD - 1))
        dt_pe.done(last, "raw")
        dt_dve.after(pe, "da")
        for d, (end, into) in enumerate([("gt", "le"), ("lt", "ge")]):
            heads = slice(d * N_HEADS, (d + 1) * N_HEADS)
            last = pe.matmul(end_psum[:, :, heads], cst[:, CST[end]], small[:, DA, :, heads], start=True, stop=True)
        dt_pe.done(last, "end")
        for d, (end, into) in enumerate([("gt", "le"), ("lt", "ge")]):
            heads = slice(d * N_HEADS, (d + 1) * N_HEADS)
            last = pe.matmul(into_psum[:, :, heads], cst[:, CST[into]], small[:, DA, :, heads], start=True, stop=True)
        dt_pe.done(last, "into")
        dt_pe.done(pe.matmul(over_psum, ones, small[:, DA], start=True, stop=True), "over")

        norm1.act.all(pe)
        dt_dve.all(pe)
        dt_act.all(pe)
        mods_dve.all(pe)
        with pe.Fori(0, GROUPS) as g:
            def conv_tile(m):
                if m == 0:
                    pe.wait_ge(w_loaded[0], g * 16 + (ssd_first[0] + 16))
                    ssd_act.after_last(pe, "z_silu", g)
                elif m == 1:
                    ssd_dve.after_last(pe, "masked7", g)
                else:
                    ssd_dve.after(pe, f"tap{m - 2}_4", g)
                if m == 4:
                    pe.wait_ge(w_loaded[1], g * 32 + (ssd_first[1] + 16))
                w = slot[m // 4]
                for k in range(KD):
                    for part, (c0, n) in enumerate(conv_parts(m)):
                        last = pe.matmul(ps[:, 2 * (m % 2) + part, 0:n], w[:, (k * 4 + m % 4) * P:(k * 4 + m % 4 + 1) * P],
                                         hT[:, k, c0:c0 + n], start=(k == 0), stop=(k == KD - 1))
                ssd_pe.done(last, f"conv{m}")

            def turn_tile(m):
                ssd_act.after(pe, f"silu{m}", g)
                if m >= 2:
                    ssd_act.after(pe, f"token{m - 2}", g)
                elif m == 0:
                    ssd_dve.after_last(pe, "gated3", g)
                bank = 4 + 2 * (m % 2)
                for t in range(ALLT):
                    last = pe.transpose(ps[:, bank + t // 4, (t % 4) * P:(t % 4 + 1) * P],
                                        CONV_DST[m][:, t * P:(t + 1) * P], ident)
                ssd_pe.done(last, f"turned{m}")

            conv_tile(0)
            for m in range(6):
                conv_tile(m + 1)
                turn_tile(m)
            conv_tile(7)

            def states(d):
                ssd_pool.after(pe, f"x_end{d}", g)
                ssd_act.after(pe, "token5", g)
                for i, t in enumerate(STATES[d]):
                    if i >= 2:
                        ssd_dve.after(pe, f"state{d}_{i - 2}", g)
                    elif d == 1 and i == 0:
                        ssd_dve.after(pe, "state0_4", g)
                    ssd_pe.done(pe.matmul(ps[:, 4 + i % 2, :], b_tok[:, t, d, :], x_end[:, t, :], start=True, stop=True),
                                f"state{d}_{i}")

            def segment(j):
                d, _, t = CHUNKS[j]
                ssd_pool.after(pe, f"upto{j}", g)
                if j:
                    ssd_act.after(pe, f"decay{j - 1}", g)
                else:
                    ssd_dve.after(pe, "tap7_4", g)
                for q in range(2):
                    last = pe.matmul(ps[:, q, :], cst[:, CST["lt" if d else "gt"]], da_upto[:, 4 * q:4 * q + 4, :],
                                     start=True, stop=True)
                ssd_pe.done(last, f"segment{j}")
                if j:
                    ssd_dve.after(pe, f"cb{j - 1}", g)
                else:
                    ssd_act.after(pe, "silu7", g)
                tokens = slice(t * P, (t + 1) * P)
                ssd_pe.done(pe.matmul(ps[:, 2, 0:P], bT[:, d, tokens], cT[:, d, tokens], start=True, stop=True), f"cb{j}")

            states(0)
            segment(0)
            for j in range(8):
                d, i, t = CHUNKS[j]
                if j == 4:
                    states(1)
                if j < 7:
                    segment(j + 1)
                if j == 0:
                    pe.wait_ge(w_loaded[1], g * 32 + (ssd_first[1] + 32))
                elif j % 2 == 0:
                    ssd_act.after(pe, f"z{j // 2 - 1}", g)
                for k in range(4 * (j % 2), 4 * (j % 2) + 4):
                    last = pe.matmul(ps[:, 3, :], slot[1][:, (k * 4 + j // 2) * P:(k * 4 + j // 2 + 1) * P],
                                     hT[:, k, 0:SEQ], start=(k == 0), stop=(k == KD - 1))
                if j % 2:
                    ssd_pe.done(last, f"z{j // 2}")
                ssd_dve.after(pe, f"masked{j}", g)
                ssd_pool.after(pe, f"x_dt{d}", g)
                if j:
                    ssd_dve.after(pe, f"both{j - 1}", g)
                for h in range(HPG):
                    last = pe.matmul(ps[:, 6, h * HD:(h + 1) * HD], decay[j % 2][:, h, :], x_dt[:, t, h * HD:(h + 1) * HD],
                                     start=True, stop=True)
                ssd_pe.done(last, f"diagonal{j}")
                ssd_dve.after(pe, f"state{d}_{i + 1}", g)
                ssd_pe.done(pe.matmul(ps[:, 7, :], cT[:, d, t * P:(t + 1) * P], state[:, i, :], start=True, stop=True),
                            f"carried{j}")
            ssd_dve.after(pe, "y7", g)
            for m in range(4):
                if m >= 2:
                    ssd_dve.after(pe, f"gated{m - 2}", g)
                for t in range(TT):
                    last = pe.transpose(ps[:, 4 + m % 2, t * P:(t + 1) * P], y_tok[:, t, m * P:(m + 1) * P], ident)
                ssd_pe.done(last, f"yT{m}")

        norm_y.on_pe(pe)
        ssd_out.multiply(pe, ready=norm_y.ready_on(pe))
        ssd_out.ev.all(pe)
        f_in.multiply(pe)
        f_in.ev.all(pe)
        pe.wait_ge(s_dft_dim, 16)
        for i in range(TT * 4):
            t, q = i // 4, i % 4
            if i >= 4:
                dft_act.after(pe, f"dim{i - 4}")
            for g in range(2):
                last = pe.matmul(ps[:, 4 + i % 4, g * 2 * P:(g + 1) * 2 * P], fT[:, 2 * q + g, t * P:(t + 1) * P], dft_dim[:],
                                 start=True, stop=True)
            dft_pe.done(last, f"dim{i}")
        pe.wait_ge(s_dft_seq, 16)
        dft_act.after(pe, "dim15")
        for g in range(FG):
            if g >= 4:
                dft_act.after(pe, f"seq{g - 4}")
            for t in range(TT):
                for part in range(2):
                    last = pe.matmul(ps[:, 4 + g % 4, :], f_dim[:, t, g, part * P:(part + 1) * P], dft_seq[:, t, part, :],
                                     start=(t == 0 and part == 0), stop=(t == TT - 1 and part == 1))
            dft_pe.done(last, f"seq{g}")
        gate_f.multiply(pe)
        gate_f.ev.all(pe)
        dft_act.all(pe)
        four_out.multiply(pe)
        four_out.ev.all(pe)
        gate_s.multiply(pe)
        gate_s.ev.all(pe)
        w_o.multiply(pe)

        w_o.ev.all(pe)
        norm2.on_pe(pe)
        pe.wait_ge(s_wr, 16)
        norm2_ready = norm2.ready_on(pe)
        for t in range(TT):
            for k in range(KD):
                if t == 0:
                    norm2_ready(k)
                last = pe.matmul(ps[:, 0, t * NE:(t + 1) * NE], h2T[:, k, t * P:(t + 1) * P], w_r[:, k, :], start=(k == 0), stop=(k == KD - 1))
        route_pe.done(last, "logits")

        def turn_tokens(i):
            if i >= 4:
                route_act.after(pe, f"turned{i - 4}")
            for k in range(4):
                last = pe.transpose(ps[:, 4 + i % 4, k * P:(k + 1) * P], h2T[:, (i % 2) * 4 + k, (i // 2) * P:(i // 2 + 1) * P], ident)
            route_pe.done(last, f"turned{i}")

        for i in range(TT):
            turn_tokens(i)
        route_dve.after(pe, "assigned")
        for t in range(TT):
            pe.matmul(ps[:, 1, t * NE:(t + 1) * NE], cst[:, CST["lt"]], assigned[:, t, :], start=True, stop=(t == 0))
            for u in range(t):
                pe.matmul(ps[:, 1, t * NE:(t + 1) * NE], ones, assigned[:, u, :], start=False, stop=(u == t - 1))
        for t in range(TT):
            last = pe.matmul(ps[:, 1, TT * NE:(TT + 1) * NE], ones, assigned[:, t, :], start=(t == 0), stop=(t == TT - 1))
        route_pe.done(last, "ranks")
        for i in range(TT, 2 * TT):
            turn_tokens(i)

        route_dve.after(pe, "n_blocks")
        n = pe.value_load(n_blocks[0:1, 0:1], min_val=1, max_val=BLOCKS)

        def turn_rows():
            for k in range(KD):
                last = pe.transpose(ps[:, 4 + k // 4, (k % 4) * P:(k % 4 + 1) * P], x_row[:, k * P:(k + 1) * P], ident)
            return last

        pe.wait_ge(s_xrow, 16)
        route_act.all(pe)
        x0_pe.done(turn_rows(), "xT")
        x0_act.all(pe)
        with pe.Fori(0, n) as i:
            def turn_act(j):
                moe_dve.after(pe, f"act{j}", i)
                for k in range(4):
                    last = pe.transpose(ps[:, j, k * P:(k + 1) * P], gate[j][:, k * P:(k + 1) * P], ident)
                moe_pe.done(last, f"aT{j}")

            def down(j, k):
                for h in range(2):
                    last = pe.matmul(ps[:, 6 + h, :], aT[:, 4 * j + k, :], slot[4 + j][:, k * D + h * 512:k * D + (h + 1) * 512],
                                     start=(j == 0 and k == 0), stop=(j == 1 and k == 3))
                return last

            for c, name in enumerate(["gate0", "up0", "gate1", "up1"]):
                pe.wait_ge(w_loaded[c], i * 16 + (exp_first[c] + 16))
                if c == 0:
                    moe_act.after_last(pe, "xT", i)
                if c < 2:
                    moe_act.after_last(pe, f"aT{c}", i)
                else:
                    moe_dve.after_last(pe, name, i)
                for k in range(KD):
                    last = pe.matmul(ps[:, c, :], xT_blk[:, k, :], slot[c][:, k * 512:(k + 1) * 512], start=(k == 0), stop=(k == KD - 1))
                moe_pe.done(last, name)
                if name == "gate1":
                    turn_act(0)
            pe.wait_ge(s_xrow, i * 16 + 32)
            moe_pe.done(turn_rows(), "xT")
            moe_act.after(pe, "aT0", i)
            pe.wait_ge(w_loaded[4], i * 16 + (exp_first[4] + 16))
            moe_act.after_last(pe, "y", i)
            for k in range(4):
                if k == 2:
                    turn_act(1)
                last = down(0, k)
            moe_pe.done(last, "down0")
            moe_act.after(pe, "aT1", i)
            pe.wait_ge(w_loaded[5], i * 16 + (exp_first[5] + 16))
            for k in range(4):
                last = down(1, k)
            moe_pe.done(last, "down1")

        pe.wait_ge(moe_act.sem, n * moe_act.n + moe_act.first)
        for t in range(TT):
            last = pe.transpose(ps[0:NE, 4, t * P:(t + 1) * P], weight[:, t, :], ident)
        back_pe.done(last, "weightT")
        back_act.all(pe)
        pe.wait_ge(s_bdn, 16)
        for t in range(TT):
            if t:
                back_dve.after(pe, f"bias{t - 1}")
            for h in range(2):
                last = pe.matmul(ps[:, h, :], weightT[:, t, :], b_dn[:, h * 512:(h + 1) * 512], start=True, stop=True)
            back_pe.done(last, f"bias{t}")
            back_dve.after(pe, f"bias{t}")
            if t:
                back_dve.after(pe, f"x2{t - 1}")
            for k in range(KD):
                last = pe.transpose(ps[:, 2 + k // 4, (k % 4) * P:(k % 4 + 1) * P], moe_tok[t % 2][:, k * P:(k + 1) * P], ident)
            back_pe.done(last, f"turned{t}")

        final.on_pe(pe)
        norm1_2.on_pe(pe)
        pe.wait_ge(s_rope, 16)
        q_rot.pe.open(pe)

        def q_besides(j, it):
            if j >= 1:
                q_rot.on_pe(pe, j - 1, it)
            if j == q_in.n - 1:
                q_rot.on_pe(pe, j, it)

        q_in.multiply(pe, q_besides, ready=norm1_2.ready_on(pe))
        q_in.ev.all(pe)
        k_rot.pe.open(pe)
        q_rot.dve.all(pe)

        def kv_besides(j, it):
            if 1 <= j <= NKV:
                k_rot.on_pe(pe, j - 1, it)
            if j == kv_in.n - 1:
                k_rot.act.all(pe)
                k_rot.dve.all(pe)
                kv_in.ev.all(pe)
                for v in range(NKV):
                    for t in range(NQT):
                        last = pe.transpose(ps[0:QT, 4 + 2 * v + t // 3, (t % 3) * P:(t % 3 + 1) * P],
                                            vT[v][:].rearrange("p a c -> p (a c)")[:, t * QT:(t + 1) * QT], ident)
                    v_pe.done(last, f"turned{v}")

        kv_in.multiply(pe, kv_besides)

        attn_pe.open(pe)
        k_rot.dve.all(pe)
        v_act.all(pe)

        def turn_probs(t, it):
            attn_dve.after(pe, f"inverse{t}", it)
            if t >= 2:
                attn_dve.after(pe, f"turned{t - 2}", it)
            for k in NT:
                last = pe.matmul(ps[0:QT, 4 + 2 * (t % 2) + k // 3, (k % 3) * QT:(k % 3 + 1) * QT],
                                 probs[t % 2][:].rearrange("p a c -> p (a c)")[:, k * QT:(k + 1) * QT], inverse_of[t % 2][:],
                                 start=True, stop=True)
            attn_pe.done(last, f"turned{t}")

        def scores(t, kv):
            for p in range(2):
                last = pe.matmul(ps[0:QT, 2 * (t % 2) + p, 0:H2], q_now[:, t * QT:(t + 1) * QT],
                                 kT[:, kv, p * H2:(p + 1) * H2], start=True, stop=True)
            return last

        first_dve.after(pe, "q")
        for kv in range(NKV):
            if kv:
                attn_dve.after(pe, "out", kv * QPK - 1)
            first_pe.done(scores(0, kv), "scores")
            with pe.Fori(0, QPK) as h:
                it = h + kv * QPK
                for t in range(1, NQT):
                    if t >= 2:
                        attn_act.after(pe, f"exp{t - 2}", it)
                    attn_pe.done(scores(t, kv), f"scores{t}")
                    if t == LAG:
                        attn_dve.after_last(pe, "out", it)
                    if t >= LAG:
                        turn_probs(t - LAG, it)
                attn_dve.after(pe, "q_next", it)
                attn_act.after(pe, f"exp{NQT - 2}", it)
                attn_pe.done(scores(0, kv), "scores_next")
                for t in range(NQT - LAG, NQT):
                    turn_probs(t, it)
                attn_dve.after(pe, f"turned{NQT - 1}", it)
                for k in NT:
                    for p in range(2):
                        last = pe.matmul(ps[:, 4 + p, 0:H2], v_tok[:, kv, k, :], probsT[:, k, p * H2:(p + 1) * H2],
                                         start=(k == 0), stop=(k == NQT - 1))
                attn_pe.done(last, "out")

        rg_pe.open(pe)
        attn_dve.all(pe)

        def rg_gates(j, it):
            if j not in (1, 2):
                return
            d = j - 1
            if d == 0:
                pe.wait_ge(s_rg, it * 16 + 16)
                rg_dve.after(pe, f"conv{CONV_W - 1}", it)
                rg_act.after_last(pe, "i1", it)
            else:
                rg_act.after(pe, "i0", it)
            for g in range(2):
                for p in range(2):
                    last = pe.matmul(ps[:, 4 + 2 * g + p, 0:H2], slot[5][:, (2 * d + g) * P:(2 * d + g + 1) * P],
                                     xcv[:, p * H2:(p + 1) * H2], start=True, stop=True)
            rg_pe.done(last, f"gates{d}")

        rnn_in.multiply(pe, rg_gates)

        rnn_in.ev.all(pe)
        out2.multiply(pe, ready=lambda k: rg_dve.after(pe, "out", k))
        norm2_2.on_pe(pe)
        ffn_in.multiply(pe, ready=norm2_2.ready_on(pe))
        ffn_in.ev.all(pe)
        ffn_out.multiply(pe)

    @block.vector
    def _(dve):
        dve.wait_ge(s_x, 16)
        norm1.invert(dve)
        mods_pe.after(dve, f"rows{MOD_CHUNKS - 1}")
        mods_dve.done(dve.tensor_copy(mod_row[:], ps[0:2, 0:MOD_CHUNKS, :]), "rows")
        dve.wait_ge(s_prm, 16)
        mods_pe.after(dve, "turned")
        mods_dve.done(dve.tensor_tensor(mod[:, 0:MOD_FIRST, :].rearrange("p m c -> p (m c)"), ps[:, 6, 0:2 * MOD_FIRST],
                                        prm[:, PRM["b_mod"].start:PRM["b_mod"].start + 2 * MOD_FIRST], ALU.add), "bias")
        mods_dve.after(dve, "bias")
        scale1.done(dve.tensor_scalar(mod_scale[:], mod[:, KD:2 * KD, :], 1.0, None, ALU.add), "plus1")
        scale1.after(dve, "plus1")
        scale1.done(dve.tensor_tensor(mod_scale[:], mod_scale[:],
                                      prm[:, PRM["norm1"]].unsqueeze(2).broadcast_to([P, KD, 2]), ALU.mult), "times")
        scale1.after(dve, "times")
        norm1.scale(dve)

        dt_pe.after(dve, "raw")
        dt_dve.done(dve.tensor_tensor(dt_raw[:], dt_psum, prm[:, PRM["dt_bias"]].unsqueeze(1).broadcast_to([P, ALLT, 2 * N_HEADS]),
                                      ALU.add), "raw")
        dt_act.after(dve, "ln")
        dt_dve.done(dve.scalar_tensor_tensor(out=small[:, DT], in0=dt_raw[:], scalar=0.0, in1=soft[:],
                                             op0=ALU.max, op1=ALU.add), "dt")
        dt_dve.after(dve, "dt")
        dt_dve.done(dve.scalar_tensor_tensor(out=small[:, DA], in0=small[:, DT], scalar=-1.0,
                                             in1=exp_a[:].unsqueeze(1).broadcast_to([P, ALLT, 2 * N_HEADS]),
                                             op0=ALU.mult, op1=ALU.mult), "da")
        dt_act.after(dve, "end")
        dt_dve.done(dve.tensor_tensor(small[:, DT_END], small[:, DT_END], small[:, DT], ALU.mult), "end")

        ssd_dve.open(dve)
        dt_dve.all(dve)
        dt_act.all(dve)
        with dve.Fori(0, GROUPS) as g:
            ssd_act.after_last(dve, "silu7", g)
            ssd_pool.after_last(dve, "upto7", g)
            ssd_dve.done(dve.tensor_scalar(
                g_small[:].rearrange("p k t d h -> p (k t d) h"),
                small[:].rearrange("p k t (d h) -> p (k t d) h", d=2)[:, :, bass.ds(g * HPG, HPG)],
                1.0, None, ALU.mult), "g_small")
            ssd_dve.done(dve.tensor_scalar(
                g_conv[:].rearrange("p m k -> p (m k)"),
                prm[:, bass.ds(g * (8 * (CONV_K + 1)) + PRM["conv"].start, 8 * (CONV_K + 1))], 1.0, None, ALU.mult), "g_conv")
            ssd_dve.done(dve.tensor_scalar(g_skip[:], prm[:, bass.ds(g * HPG + PRM["d_skip"].start, HPG)], 1.0, None, ALU.mult),
                         "g_skip")
            ssd_dve.after(dve, "g_skip", g)
            for m in range(8):
                for k in TAPS:
                    if k == 0:
                        ssd_act.after(dve, f"centre{m}", g)
                    else:
                        ssd_dve.after(dve, f"tap{m}_{TAPS[TAPS.index(k) - 1]}", g)
                    off = k - CONV_K // 2
                    for part, (c0, n) in enumerate(conv_parts(m)):
                        lo, hi = max(0, -off), min(n, n - off)
                        last = dve.scalar_tensor_tensor(
                            out=conv[:, c0 + lo:c0 + hi], in0=ps[:, 2 * (m % 2) + part, lo + off:hi + off],
                            scalar=g_conv[:, m, k:k + 1], in1=conv[:, c0 + lo:c0 + hi], op0=ALU.mult, op1=ALU.add)
                    ssd_dve.done(last, f"tap{m}_{k}")

            def fade(d, src, tile, name):
                ssd_dve.done(dve.tensor_tensor(by_head(y_part[:]), by_head(src), per_head(OVER, tile, d), ALU.mult), name)

            def states(d):
                order = STATES[d]
                ssd_pe.after(dve, f"state{d}_0", g)
                fade(d, ps[:, 4, :], order[1], f"state{d}_0")
                for i in range(1, 5):
                    if i >= 2:
                        ssd_dve.after(dve, f"state{d}_{i - 1}", g)
                        fade(d, state[:, i - 2, :], order[i], f"faded{d}_{i}")
                        ssd_dve.after(dve, f"faded{d}_{i}", g)
                    else:
                        ssd_dve.after(dve, f"state{d}_0", g)
                    ssd_pe.after(dve, f"state{d}_{i}", g)
                    ssd_dve.done(dve.tensor_tensor(state[:, i - 1, :], y_part[:], ps[:, 4 + i % 2, :], ALU.add), f"state{d}_{i}")

            def mask(j):
                d = CHUNKS[j][0]
                ssd_pe.after(dve, f"cb{j}", g)
                ssd_dve.done(dve.tensor_tensor(cb_masked[j % 2][:], ps[:, 2, 0:P], cst[:, CST["ge" if d else "le"]], ALU.mult), f"cb{j}")
                ssd_dve.after(dve, f"cb{j}", g)
                ssd_act.after(dve, f"decay{j}", g)
                ssd_dve.done(dve.tensor_tensor(decay[j % 2][:], decay[j % 2][:],
                                               cb_masked[j % 2][:].unsqueeze(1).broadcast_to([P, HPG, P]), ALU.mult), f"masked{j}")

            states(0)
            mask(0)
            for j in range(8):
                d, i, t = CHUNKS[j]
                if j == 4:
                    ssd_dve.after(dve, "y3", g)
                    states(1)
                if j < 7:
                    mask(j + 1)
                ssd_dve.after(dve, {0: "state0_4", 4: "state1_4"}.get(j, f"y{j - 1}"), g)
                ssd_pe.after(dve, f"carried{j}", g)
                ssd_dve.done(dve.tensor_tensor(by_head(y_part[:]), by_head(ps[:, 7, :]), per_head(INTO, t, d), ALU.mult), f"carried{j}")
                ssd_dve.after(dve, f"carried{j}", g)
                ssd_dve.done(dve.tensor_tensor(y_part[:], y_part[:], ps[:, 6, :], ALU.add), f"both{j}")
                ssd_dve.after(dve, f"both{j}", g)
                ssd_pool.after(dve, "skip", g)
                ssd_dve.done(dve.tensor_tensor(y_tok[:, t, :], y_tok[:, t, :], y_part[:], ALU.add), f"y{j}")
            ssd_act.after(dve, "z_silu", g)
            for m in range(4):
                ssd_pe.after(dve, f"yT{m}", g)
                out = gate_yT[:].rearrange("p k t -> p (k t)")[:, bass.ds(g * (4 * SEQ) + m * SEQ, SEQ)]
                ssd_dve.done(dve.tensor_tensor(out, ps[:, 4 + m % 2, :], zT[:, m, :], ALU.mult), f"gated{m}")

        norm_y.on_dve(dve)
        four_out.ev.open(dve)
        gate_s.ev.open(dve)
        w_o.ev.open(dve)
        late_dve.open(dve)
        norm_y.pe.all(dve)
        c_row_silu.all(dve)
        with dve.Fori(0, LATE) as r:
            dve.wait_ge(s_modT, r * 16 + 16)
            late_dve.after_last(dve, "bias", r)
            late_dve.done(dve.tensor_tensor(w_modT[:], w_modT[:], c_row[:], ALU.mult), "product")
            late_dve.after(dve, "product", r)
            late_dve.done(dve.tensor_reduce(mod_sum[:], w_modT[:], AX.X, ALU.add), "sum")
            late_dve.after(dve, "sum", r)
            late_dve.done(dve.tensor_tensor(mod[:].rearrange("p m c -> p (m c)")[:, bass.ds(r * 2 + 2 * MOD_FIRST, 1)], mod_sum[:],
                                            prm[:, bass.ds(r * 2 + (PRM["b_mod"].start + 2 * MOD_FIRST), 1)], ALU.add), "bias")
        late_dve.all(dve)
        gate_f.ev.all(dve)
        for j in range(four_out.n):
            four_out.pe.after(dve, f"tile{j}")
            four_out.ev.done(dve.tensor_tensor(mixT[:, j, :], four_out.bank(j, 0), gate_fT[:, j, :], ALU.mult), f"tile{j}")
        ssd_out.ev.all(dve)
        four_out.ev.all(dve)
        for j in range(gate_s.n):
            gate_s_act.after(dve, f"sigmoid{j}")
            mix_dve.done(dve.tensor_tensor(y_ssdT[:, j, :], y_ssdT[:, j, :], gate_sT[j % 2][:], ALU.mult), f"gated{j}")
            mix_dve.after(dve, f"gated{j}")
            gate_s.ev.done(dve.tensor_tensor(mixT[:, j, :], mixT[:, j, :], y_ssdT[:, j, :], ALU.add), f"tile{j}")
        dve.wait_ge(s_x1, 16)
        for j in range(w_o.n):
            w_o.pe.after(dve, f"tile{j}")
            w_o.ev.done(dve.scalar_tensor_tensor(out=x1T[:, j, :], in0=w_o.bank(j, 0), scalar=mod[:, 2 * KD + j, 0:1],
                                                 in1=x1T[:, j, :], op0=ALU.mult, op1=ALU.add), f"tile{j}")

        w_o.ev.all(dve)
        scale2_dve.done(dve.tensor_scalar(scale2[:], mod[:, 4 * KD:5 * KD, 0], 1.0, None, ALU.add), "plus1")
        scale2_dve.after(dve, "plus1")
        scale2_dve.done(dve.tensor_tensor(scale2[:], scale2[:], prm[:, PRM["norm2"]], ALU.mult), "times")
        scale2_dve.after(dve, "times")
        norm2.on_dve(dve)

        def step(name, instruction):
            route_dve.done(instruction, name)
            route_dve.after(dve, name)

        route_pe.after(dve, "logits")
        step("logits", dve.tensor_tensor(logits[:], ps[:, 0, 0:TT * NE].rearrange("p (t e) -> p t e", e=NE),
                                         prm[:, PRM["b_router"]].unsqueeze(1).broadcast_to([P, TT, NE]), ALU.add))
        for t in range(TT):
            step(f"top{t}", dve.max(top[:, t, :], logits[:, t, :]))
        for t in range(TT):
            step(f"index{t}", dve.max_index(top_i[:, t, :], top[:, t, :], logits[:, t, :]))
        step("minus_max", dve.tensor_tensor(top_e[:], top[:, :, 0:TOPK], top[:, :, 0:1].broadcast_to([P, TT, TOPK]), ALU.subtract))
        step("expert", dve.tensor_copy(top_f[:], top_i[:, :, 0:TOPK]))
        flat = picked[:].rearrange("p t k e -> p (t k) e")
        flat2 = picked2[:].rearrange("p t k e -> p (t k) e")

        def over_experts(v):
            return v.rearrange("p t k -> p (t k)").unsqueeze(2).broadcast_to([P, TT * TOPK, NE])

        step("picked", dve.tensor_tensor(flat, cst[:, CST["expert"]].unsqueeze(1).broadcast_to([P, TT * TOPK, NE]),
                                         over_experts(top_f[:]), ALU.is_equal))
        step("assigned", dve.tensor_reduce(assigned[:], picked[:].rearrange("p t k e -> p t e k"), AX.X, ALU.add))
        route_pe.after(dve, "ranks")
        count = ps[:, 1, TT * NE:(TT + 1) * NE]
        step("n0", dve.tensor_scalar(n_of[:], count, 0.0, None, ALU.is_gt))
        for b in range(1, TT):
            step(f"n{b}", dve.scalar_tensor_tensor(out=n_of[:], in0=count, scalar=float(b * P), in1=n_of[:], op0=ALU.is_gt, op1=ALU.add))
        step("end", dve.tensor_tensor_scan(end_of[:], ones[:, 0:NE], n_of[:], 0.0, ALU.mult, ALU.add))
        step("start", dve.tensor_tensor(start_of[:], end_of[:], n_of[:], ALU.subtract))
        step("row_of", dve.scalar_tensor_tensor(out=row_of[:], in0=start_of[:].unsqueeze(1).broadcast_to([P, TT, NE]), scalar=float(P),
                                                in1=ps[:, 1, 0:TT * NE].rearrange("p (t e) -> p t e", e=NE), op0=ALU.mult, op1=ALU.add))
        step("picked_row", dve.tensor_tensor(picked2[:], picked[:], row_of[:].unsqueeze(2).broadcast_to([P, TT, TOPK, NE]), ALU.mult))
        step("row", dve.tensor_reduce(row_f[:], flat2, AX.X, ALU.add))
        step("row_u", dve.tensor_copy(row_u[:], row_f[:]))
        step("ended", dve.tensor_tensor(ended[:], cst[:, CST["block"]].unsqueeze(2).broadcast_to([P, BLOCKS_IN, NE]),
                                        end_of[:].unsqueeze(1).broadcast_to([P, BLOCKS_IN, NE]), ALU.is_ge))
        step("expert_f", dve.tensor_reduce(expert_f[:], ended[:], AX.X, ALU.add))
        step("expert_of", dve.tensor_scalar(expert_of[:], expert_f[:], float(NE - 1), None, ALU.min))
        step("n_blocks", dve.tensor_copy(n_blocks[:], end_of[:, NE - 1:NE]))
        route_act.after(dve, "exp")
        step("sum", dve.tensor_reduce(top_sum[:], top_e[:], AX.X, ALU.add))
        step("inverse", dve.reciprocal(top_sum[:], top_sum[:]))
        step("top_w", dve.tensor_tensor(top_w[:], top_e[:], top_sum[:].unsqueeze(2).broadcast_to([P, TT, TOPK]), ALU.mult))
        step("picked_w", dve.tensor_tensor(flat2, flat, over_experts(top_w[:]), ALU.mult))
        step("weight", dve.tensor_reduce(weight[:], picked2[:].rearrange("p t k e -> p t e k"), AX.X, ALU.add))

        moe_dve.open(dve)
        dve.wait_ge(s_placed, 16 * TT * TOPK)
        n = dve.value_load(n_blocks[0:1, 0:1], min_val=1, max_val=BLOCKS)
        with dve.Fori(0, n) as i:
            dve.wait_ge(s_brow, i * 16 + 16)
            for j in range(2):
                moe_pe.after(dve, f"gate{j}", i)
                moe_dve.done(dve.tensor_tensor(gate[j][:], ps[:, 2 * j, :], b_row[:, 0, j * 512:(j + 1) * 512], ALU.add), f"gate{j}")
                moe_pe.after(dve, f"up{j}", i)
                moe_dve.done(dve.tensor_tensor(up[j][:], ps[:, 2 * j + 1, :], b_row[:, 1, j * 512:(j + 1) * 512], ALU.add), f"up{j}")
                moe_dve.after(dve, f"gate{j}", i)
                moe_dve.done(dve.tensor_scalar(gate[j][:], gate[j][:], SWIGLU_LIMIT, None, ALU.min), f"gate_min{j}")
                moe_dve.after(dve, f"up{j}", i)
                moe_dve.done(dve.tensor_scalar(up[j][:], up[j][:], SWIGLU_LIMIT, -SWIGLU_LIMIT, ALU.min, ALU.max), f"up_clip{j}")
                moe_dve.after(dve, f"up_clip{j}", i)
                moe_act.after(dve, f"sigmoid{j}", i)
                moe_dve.done(dve.scalar_tensor_tensor(out=gate[j][:], in0=up[j][:], scalar=1.0, in1=gate[j][:],
                                                      op0=ALU.add, op1=ALU.mult), f"times{j}")
                moe_dve.after(dve, f"times{j}", i)
                moe_dve.done(dve.tensor_tensor(gate[j][:], gate[j][:], sig[j][:], ALU.mult), f"act{j}")

        def add_back(t):
            back_pe.after(dve, f"turned{t}")
            for k in range(KD):
                last = dve.scalar_tensor_tensor(out=x1T[:, k, t * P:(t + 1) * P], in0=ps[:, 2 + k // 4, (k % 4) * P:(k % 4 + 1) * P],
                                                scalar=mod[:, 5 * KD + k, 0:1], in1=x1T[:, k, t * P:(t + 1) * P],
                                                op0=ALU.mult, op1=ALU.add)
            back_dve.done(last, f"x2{t}")

        for t in range(TT):
            dve.wait_ge(s_rows[t % 2], 16 * TOPK * (t // 2 + 1))
            acc, rows = moe_tok[t % 2], picked_rows[t % 2]
            if t >= 2:
                back_pe.after(dve, f"turned{t - 2}")
            back_dve.done(dve.tensor_scalar(acc[:], rows[:, 0, :], top_w[:, t, 0:1], None, ALU.mult), f"add{t}_0")
            for k in range(1, TOPK):
                back_dve.after(dve, f"add{t}_{k - 1}")
                back_dve.done(dve.scalar_tensor_tensor(out=acc[:], in0=rows[:, k, :], scalar=top_w[:, t, k:k + 1], in1=acc[:],
                                                       op0=ALU.mult, op1=ALU.add), f"add{t}_{k}")
            back_dve.after(dve, f"add{t}_{TOPK - 1}")
            back_pe.after(dve, f"bias{t}")
            back_dve.done(dve.tensor_tensor(acc[:].rearrange("p (h c) -> p h c", h=2), acc[:].rearrange("p (h c) -> p h c", h=2),
                                            ps[:, 0:2, :], ALU.add), f"bias{t}")
            if t:
                add_back(t - 1)
        add_back(TT - 1)

        back_dve.all(dve)
        final.on_dve(dve)
        final.dve.all(dve)
        dve.wait_ge(s_meta, 16)
        lam_dve.done(dve.tensor_copy(rnn_prm[:].rearrange("p n c -> p (n c)"), prm[:, PRM["rnn"]]), "copy")
        norm1_2.on_dve(dve)
        lam_act.after(dve, "ln")
        lam_dve.done(dve.scalar_tensor_tensor(out=lam, in0=lam, scalar=0.0, in1=lam_abs[:], op0=ALU.min, op1=ALU.subtract), "min")
        lam_dve.after(dve, "min")
        lam_dve.done(dve.tensor_scalar(lam, lam, RG_C, None, ALU.mult), "times")
        norm1_2.dve.all(dve)
        dve.wait_ge(s_rope, 16)
        q_rot.dve.open(dve)
        with rounds(dve, q_in.rounds) as it:
            for j in range(q_in.n):
                q_rot.on_dve(dve, j, it)
        q_rot.dve.all(dve)
        k_rot.dve.open(dve)
        for j in range(NKV):
            k_rot.on_dve(dve, j, 0)

        attn_dve.open(dve)
        k_rot.dve.all(dve)
        v_pe.all(dve)

        def take_turned(t, it):
            attn_pe.after(dve, f"turned{t}", it)
            attn_dve.done(dve.tensor_copy(probsT[:, :, t * QT:(t + 1) * QT].rearrange("p (a k) c -> p a k c", a=2),
                                          ps[0:QT, 4 + 2 * (t % 2):6 + 2 * (t % 2), 0:3 * QT].rearrange("p a (k c) -> p a k c", k=3)),
                          f"turned{t}")

        def take_q(head):
            return dve.tensor_scalar(q_now[:], attn_flat[:, head], cst[:, CST["one"]], None, ALU.mult)

        def take_max(t):
            return dve.tensor_reduce(row_max[:, t:t + 1], ps[0:QT, 2 * (t % 2):2 * (t % 2) + 2, 0:H2], AX.XY, ALU.max)

        def minus_max(t):
            return dve.tensor_scalar(row_max[:, t:t + 1], row_max[:, t:t + 1], -HEAD_SCALE, None, ALU.mult)

        dve.wait_ge(s_ninth, 1)
        first_dve.done(take_q(slice(0, T2)), "q")
        for kv in range(NKV):
            first_pe.after(dve, "scores", kv)
            first_dve.done(take_max(0), f"max{kv}")
            first_dve.after(dve, f"max{kv}")
            first_dve.done(minus_max(0), f"minus{kv}")
            with dve.Fori(0, QPK) as h:
                it = h + kv * QPK
                for t in NT:
                    if t:
                        attn_pe.after(dve, f"scores{t}", it)
                        if t == NQT - 1:
                            attn_dve.done(take_q(bass.ds(it * T2 + T2, T2)), "q_next")
                        attn_dve.done(take_max(t), f"max{t}")
                        attn_dve.after(dve, f"max{t}", it)
                        attn_dve.done(minus_max(t), f"minus{t}")
                    if t >= LAG:
                        take_turned(t - LAG, it)
                    attn_act.after(dve, f"exp{t}", it)
                    attn_dve.done(dve.reciprocal(row_sum[:, t:t + 1], row_sum[:, t:t + 1]), f"sum{t}")
                    attn_dve.after(dve, f"sum{t}", it)
                    attn_dve.done(dve.tensor_scalar(inverse_of[t % 2][:], cst[0:QT, 0:QT], row_sum[:, t:t + 1], None, ALU.mult),
                                  f"inverse{t}")
                for t in range(NQT - LAG, NQT):
                    take_turned(t, it)
                attn_dve.done(take_max(0), "max_next")
                attn_dve.after(dve, "max_next", it)
                attn_dve.done(minus_max(0), "minus_next")
                attn_pe.after(dve, "out", it)
                attn_dve.done(dve.tensor_scalar(attn_flat[:, bass.ds(it * T2, T2)].rearrange("p (a c) -> p a c", a=2),
                                                ps[:, 4:6, 0:H2], cst[:, CST["one"]], None, ALU.mult), "out")

        rg_dve.open(dve)
        out2.ev.open(dve)
        ffn_in.ev.open(dve)
        attn_dve.all(dve)
        dve.wait_ge(s_pad, 2)
        lam_dve.all(dve)
        rnn_flat = rnn_prm[:].rearrange("p n c -> p (n c)")
        with rounds(dve, RNN_BLOCKS) as it:
            rg_act.after_last(dve, "sqrt1", it)
            rg_dve.done(dve.tensor_scalar(one_prm[:], rnn_flat[:, bass.ds(it * 12, 12)], cst[:, CST["one"]], None, ALU.mult), "params")

            def step(name, instruction):
                rg_dve.done(instruction, name)
                rg_dve.after(dve, name, it)

            rg_dve.after(dve, "params", it)
            rnn_in.ev.after(dve, "tile0", it)
            rg_pe.after_last(dve, "gates1", it)
            step("conv0", dve.tensor_scalar(xcv[:], x_pad[:, 0:T2], one_prm[:, 0:1], one_prm[:, 4:5], ALU.mult, ALU.add))
            for j in range(1, CONV_W):
                step(f"conv{j}", dve.scalar_tensor_tensor(out=xcv[:], in0=x_pad[:, j:j + T2], scalar=one_prm[:, j:j + 1], in1=xcv[:],
                                                          op0=ALU.mult, op1=ALU.add))
            rnn_in.ev.after(dve, "tile1", it)
            step("gelu_square", dve.tensor_tensor(gelu_in[:], gr[:], gr[:], ALU.mult))
            step("cube", dve.tensor_scalar(gelu_in[:], gelu_in[:], GELU_CUBE, 1.0, ALU.mult, ALU.add))
            step("gelu_in", dve.tensor_tensor(gelu_in[:], gelu_in[:], gr[:], ALU.mult))
            rg_act.after(dve, "gelu", it)
            step("gelu", dve.tensor_tensor(gr[:], gr[:], gelu_in[:], ALU.mult))
            for d in range(2):
                rg_act.after(dve, f"i{d}", it)
                rg_dve.done(dve.tensor_tensor(i_gate[d][:], i_gate[d][:], xcv[:], ALU.mult), f"ix{d}")
                if d == 0:
                    head = attn_flat[:, bass.ds(it * T2, T2)]
                    rnn_in.ev.after(dve, "tile2", it)
                    rg_dve.done(dve.tensor_tensor(merge_attn[:], merge_attn[:], head, ALU.mult), "attn")
            for d in range(2):
                rg_act.after(dve, f"tanh{d}", it)
                rg_pool.after(dve, f"square{d}", it)
                step(f"ratio{d}", dve.scalar_tensor_tensor(out=r_gate[d][:], in0=hidden[d][:], scalar=1.0, in1=r_gate[d][:],
                                                           op0=ALU.add, op1=ALU.mult))
            for d in range(2):
                rg_act.after(dve, f"sqrt{d}", it)
                step(f"input{d}", dve.tensor_tensor(i_gate[d][:], i_gate[d][:], r_gate[d][:], ALU.mult))
                def run(t):
                    return t[:, ::-1] if d else t[:]
                step(f"scan{d}", dve.tensor_tensor_scan(run(hidden[d]), run(rg_decay[d]), run(i_gate[d]), 0.0, ALU.mult, ALU.add))
            step("both", dve.tensor_tensor(hidden[0][:], hidden[0][:], hidden[1][:], ALU.add))
            rg_pool.after(dve, "gelued", it)
            step("merged", dve.tensor_tensor(hidden[0][:], hidden[0][:], gr[:], ALU.mult))
            step("out", dve.tensor_tensor(attn_flat[:, bass.ds(it * T2, T2)], merge_attn[:], hidden[0][:], ALU.add))

        for j in range(out2.n):
            out2.pe.after(dve, f"tile{j}")
            out2.ev.done(dve.tensor_tensor(halves(h2nd[:, j, :]), halves(h2nd[:, j, :]), ps[:, 2 * (j % 2):2 * (j % 2) + 2, 0:H2],
                                           ALU.add), f"tile{j}")
        out2.ev.all(dve)
        norm2_2.on_dve(dve)
        out2.pe.all(dve)
        with rounds(dve, ffn_in.rounds) as it:
            for i in range(2):
                ffn_sig.after(dve, f"gate{i}", it)
                ffn_in.ev.done(dve.tensor_tensor(halves(ffn_gate[i][:]), halves(ffn_gate[i][:]), ps[:, 0:2, 0:H2], ALU.mult), f"tile{2 * i}")
                ffn_in.ev.after(dve, f"tile{2 * i}", it)
                ffn_in.pe.after(dve, f"tile{2 * i + 1}", it)
                ffn_in.ev.done(dve.tensor_tensor(halves(ffn_flat[:, bass.ds(it * (2 * T2) + i * T2, T2)]), halves(ffn_gate[i][:]),
                                                 ps[:, 2:4, 0:H2], ALU.mult), f"tile{2 * i + 1}")
        ffn_out.ev.open(dve)
        with rounds(dve, ffn_out.rounds) as it:
            for i in range(2):
                ffn_out.pe.after(dve, f"tile{i}", it)
                dve.wait_ge(s_out[i], it * 16 + 16)
                ffn_out.ev.done(dve.tensor_tensor(halves(y_out[i][:]), halves(h2nd_flat[:, bass.ds(it * (2 * T2) + i * T2, T2)]),
                                                  ps[:, 2 * i:2 * i + 2, 0:H2], ALU.add), f"tile{i}")

    @block.gpsimd
    def _(pool):
        pool.memset(zero[:], 0.0).then_inc(s_zero, 1)

        ssd_pool.open(pool)
        with pool.Fori(0, GROUPS) as g:
            def x_end_(d):
                ssd_pool.done(pool.tensor_tensor(x_end[:].rearrange("p t (h c) -> p t h c", c=HD),
                                                 x_tok[:].rearrange("p t (h c) -> p t h c", c=HD),
                                                 per_head(DT_END, slice(0, ALLT), d), ALU.mult), f"x_end{d}")

            def x_dt_(d):
                ssd_pool.done(pool.tensor_tensor(x_dt[:].rearrange("p t (h c) -> p t h c", c=HD),
                                                 x_tok[:, 0:TT].rearrange("p t (h c) -> p t h c", c=HD),
                                                 per_head(DT, slice(0, TT), d), ALU.mult), f"x_dt{d}")

            def upto(j):
                d, _, t = CHUNKS[j]
                if j:
                    ssd_pe.after(pool, f"segment{j - 1}", g)
                ssd_pool.done(pool.tensor_tensor(da_upto[:], cst[:, CST["ge" if d else "le"]].unsqueeze(1).broadcast_to([P, HPG, P]),
                                                 per_head(DA, t, d, P), ALU.mult), f"upto{j}")

            ssd_act.after(pool, "token3", g)
            ssd_dve.after(pool, "g_skip", g)
            x_end_(0)
            x_dt_(0)
            upto(0)
            ssd_pool.done(pool.tensor_tensor(y_tok[:].rearrange("p t (h c) -> p t h c", c=HD),
                                             x_tok[:, 0:TT].rearrange("p t (h c) -> p t h c", c=HD),
                                             g_skip[:].unsqueeze(1).unsqueeze(3).broadcast_to([P, TT, HPG, HD]), ALU.mult), "skip")
            upto(1)
            ssd_pe.after(pool, "state0_4", g)
            x_end_(1)
            upto(2)
            upto(3)
            upto(4)
            ssd_pe.after(pool, "diagonal3", g)
            x_dt_(1)
            upto(5)
            upto(6)
            upto(7)

        norm_y.dve.all(pool)
        norm_y.pe.all(pool)
        pool.dma_start(c_row[:], io["c_row"].partition_broadcast(P)).then_inc(s_c_row, 16)
        with pool.Fori(0, LATE) as r:
            late_dve.after_last(pool, "sum", r)
            pool.sem_inc(s_tile_free, 1)
            pool.dma_start(w_modT[:], row(io["w_modT"], r)).then_inc(s_modT, 16)

        route_dve.after(pool, "row_u")
        pool.wait_ge(s_cleared, 16 * GROUPS)
        for t in range(TT):
            route_act.after(pool, f"turned{2 * t + 1}")
            for k in range(TOPK):
                pool.indirect_dma_start(out=expert_rows, out_offset=bass.IndirectOffsetOnAxis(ap=row_u[:, t * TOPK + k:t * TOPK + k + 1], axis=0),
                                        in_=h2_tok[:, t, :], in_offset=None).then_inc(s_placed, 16)
        pool.wait_ge(s_all_stored, 1)
        back_pe.after(pool, "weightT")
        for t in range(TT):
            if t >= 2:
                back_dve.after(pool, f"add{t - 2}_{TOPK - 1}")
            for k in range(TOPK):
                pool.indirect_dma_start(out=picked_rows[t % 2][:, k, :], out_offset=None, in_=expert_rows,
                                        in_offset=bass.IndirectOffsetOnAxis(ap=row_u[:, t * TOPK + k:t * TOPK + k + 1], axis=0)
                                        ).then_inc(s_rows[t % 2], 16)

        final.dve.all(pool)
        pool.memset(attnT[:, KD, :], 0.0).then_inc(s_ninth, 1)

        attn_dve.all(pool)
        pool.memset(x_pad[:, 0:CONV_W // 2], 0.0).then_inc(s_pad, 1)
        pool.memset(x_pad[:, CONV_W // 2 + T2:], 0.0).then_inc(s_pad, 1)
        with rounds(pool, RNN_BLOCKS) as it:
            for d in range(2):
                rg_act.after(pool, f"exp{d}", it)
                rg_pool.done(pool.tensor_tensor(hidden[d][:], rg_decay[d][:], rg_decay[d][:], ALU.mult), f"square{d}")
            rnn_in.ev.after(pool, "tile3", it)
            rg_dve.after(pool, "gelu", it)
            rg_pool.done(pool.tensor_tensor(gr[:], gr[:], merge_rnn[:], ALU.mult), "gelued")

    block_scope.__exit__(None, None, None)


def shape_constants():
    f = np.float32
    cst = np.zeros((P, CST.width), f)
    a, b = np.arange(P)[:, None], np.arange(P)[None, :]
    cst[:, CST["ident"]] = a == b
    cst[:, CST["ones"]] = 1
    cst[:, CST["le"]] = a <= b
    cst[:, CST["gt"]] = a > b
    cst[:, CST["ge"]] = a >= b
    cst[:, CST["lt"]] = a < b
    cst[:, CST["expert"]] = np.arange(NE)
    cst[:, CST["block"]] = np.arange(BLOCKS + 1)
    cst[:, CST["eps"]] = EPS
    cst[:, CST["one"]] = 1
    t = np.arange(SEQ)
    angle = 2 * np.pi * ((t[:, None] * t[None, :]) % SEQ) / SEQ
    seq = np.stack([np.cos(angle), -np.sin(angle)], 1) / 256.0
    dft_seq = seq.reshape(TT, P, 2, SEQ).transpose(1, 0, 2, 3)
    angle = 2 * np.pi * ((a * b) % P) / P
    dft_dim = np.concatenate([np.cos(angle), np.sin(angle)], 1)
    pairs = P // 4
    inv = np.exp(-np.log(f(ROPE_THETA)) * np.arange(pairs, dtype=f) / f(pairs)).astype(f)
    row = np.concatenate([np.zeros(N_META), np.repeat(np.arange(SEQ // GRID_W), GRID_W)]).astype(f)
    col = np.concatenate([np.zeros(N_META), np.tile(np.arange(GRID_W), SEQ // GRID_W)]).astype(f)
    angle = np.concatenate([inv[:, None] * row, inv[:, None] * row, inv[:, None] * col, inv[:, None] * col], 0)
    rope = np.concatenate([np.cos(angle), np.sin(angle)], 1)
    turn = np.zeros((P, P), f)
    for base in (0, 2 * pairs):
        for i in range(pairs):
            turn[base + pairs + i, base + i] = -1
            turn[base + i, base + pairs + i] = 1
    return {"cst": cst, "dft_seq": np.ascontiguousarray(dft_seq).astype(f), "dft_dim": dft_dim.astype(f),
            "rope": np.concatenate([rope, turn], 1).astype(f)}


def by_channel(v, tiles):
    return np.asarray(v).reshape(tiles, P).T


def chunks(w, tiles, order=None):
    k, n = w.shape
    v = w.reshape(k // P, P, n // P, P)
    if order is not None:
        v = v[:, :, order]
    v = v.reshape(k // P, P, v.shape[2] // tiles, tiles, P).transpose(2, 1, 0, 3, 4)
    return np.ascontiguousarray(v).reshape(v.shape[0], P, -1)


def tile_chunks(w, tiles):
    k, n = w.shape
    v = w.reshape(k // P, P, n // P // tiles, tiles, P).transpose(2, 1, 3, 0, 4)
    return np.ascontiguousarray(v).reshape(v.shape[0], P, -1)


def lay_out(x, c, ctx, c_ctx, w_mod, b_mod, norm1_w, norm2_w, w_in, conv_w, conv_b, dt_bias, a_log,
            d_skip, ssd_norm_w, w_ssd_out, w_four_out, w_o, w_router, b_router, w_gate_up, b_gate_up,
            w_down, b_down, final_norm_w, meta_tokens_2, norm1_g_2, w_in_2, conv_w_2, conv_b_2, rg_wa_2,
            rg_ba_2, rg_wx_2, rg_bx_2, rg_lambda_2, q_norm_g_2, k_norm_g_2, w_out_2, norm2_g_2,
            w_ffn_in_2, w_ffn_out_2):
    out = shape_constants()
    prm = np.zeros((P, PRM.width), np.float32)
    prm[:, PRM["c"]] = np.stack([by_channel(c, KD), by_channel(c_ctx, KD)], 2).reshape(P, -1)
    prm[:, PRM["b_mod"]] = np.repeat(by_channel(b_mod, N_MOD * KD), 2, 1)
    prm[:, PRM["norm1"]] = by_channel(norm1_w, KD)
    prm[:, PRM["norm2"]] = by_channel(norm2_w, KD)
    prm[:, PRM["final"]] = by_channel(final_norm_w, KD)
    taps = np.concatenate([conv_w[0], conv_b], 0).reshape(CONV_K + 1, -1, P).transpose(2, 1, 0)
    nx, ng = D_INNER // P, GROUPS
    order = [t for g in range(GROUPS) for t in (*range(4 * g, 4 * g + 4), nx + g, nx + ng + g, nx + 2 * ng + g, nx + 3 * ng + g)]
    prm[:, PRM["conv"]] = taps[:, order].reshape(P, -1)
    prm[:, PRM["ssd_norm"]] = by_channel(ssd_norm_w, 2 * KD)
    prm[:, PRM["dt_bias"]] = dt_bias.reshape(1, -1)
    prm[:, PRM["a_log"]] = a_log.reshape(1, -1)
    prm[:, PRM["d_skip"]] = d_skip.reshape(1, -1)
    prm[:, PRM["b_router"]] = b_router.reshape(1, -1)
    prm[:, PRM["norm1_2"]] = by_channel(norm1_g_2, KD)
    prm[:, PRM["norm2_2"]] = by_channel(norm2_g_2, KD)
    rnn = np.zeros((P, RNN_BLOCKS, 12), np.float32)
    rnn[:, :, 0:4] = conv_w_2[0].reshape(CONV_W, KD, P).transpose(2, 1, 0)
    rnn[:, :, 4] = by_channel(conv_b_2, KD)
    for d in range(2):
        rnn[:, :, 6 + d] = by_channel(rg_ba_2[0, d], KD)
        rnn[:, :, 8 + d] = by_channel(rg_bx_2[0, d], KD)
        rnn[:, :, 10 + d] = by_channel(rg_lambda_2[0, d], KD)
    prm[:, PRM["rnn"]] = rnn.reshape(P, -1)
    prm[:, PRM["qk_norm"]] = np.stack([q_norm_g_2[0], k_norm_g_2[0]], 1)
    out["prm"] = prm
    rows = np.concatenate([x[0], ctx[0]], 0)
    out["xcT"] = np.ascontiguousarray(rows.T.reshape(KD, P, SEQ + CTX).transpose(1, 0, 2))
    out["metaT"] = np.ascontiguousarray(meta_tokens_2.T.reshape(KD, P, N_META).transpose(1, 0, 2))
    out["w_mod"] = chunks(w_mod[0][:, :2 * D], 4)
    out["w_modT"] = np.ascontiguousarray(w_mod[0][:, 2 * D:].T).reshape(-1, P, D)
    out["c_row"] = np.asarray(c).reshape(1, D)
    w = w_in[0]
    out["w_xbc"] = np.concatenate([chunks(np.concatenate([w[:, 0:OFF_DT], w[:, OFF_CF:OFF_Z]], 1), 4, order)], 0)
    out["w_dt"] = np.ascontiguousarray(w[:, OFF_DT:OFF_CF].reshape(KD, P, 2 * N_HEADS).transpose(1, 0, 2))
    out["w_z"] = chunks(w[:, OFF_Z:OFF_F], 4)
    out["w_f"] = chunks(w[:, OFF_F:OFF_GF], 4)
    out["w_gf"] = chunks(w[:, OFF_GF:OFF_GS], 4)
    out["w_gs"] = chunks(w[:, OFF_GS:], 4)
    out["w_ssd"] = tile_chunks(w_ssd_out[0], 2)
    out["w_four"] = chunks(w_four_out[0], 4)
    out["w_o"] = chunks(w_o[0], 4)
    out["w_router"] = np.ascontiguousarray(w_router[0].reshape(KD, P, NE).transpose(1, 0, 2))
    gu = w_gate_up[0].reshape(NE, KD, P, 2, 2, 512).transpose(0, 4, 3, 2, 1, 5).reshape(NE, 4, P, CHUNK)
    dn = w_down[0].reshape(NE, 2, 4, P, D).transpose(0, 1, 3, 2, 4).reshape(NE, 2, P, CHUNK)
    out["w_exp"] = np.concatenate([gu, dn], 1).reshape(NE * 6, P, CHUNK)
    out["b_gu"] = b_gate_up[0]
    out["b_down"] = b_down[0]
    w = w_in_2[0]
    qw = w[:, :D]
    kv = w[:, D:D + 2 * NKV * P]
    out["w_q"] = chunks(qw, 2)
    out["w_kv"] = chunks(kv, 4)
    rest = w[:, D + 2 * NKV * P:]
    out["w_rnn"] = chunks(rest, 2, [t * KD + n for n in range(KD) for t in range(4)])
    rg = np.stack([rg_wa_2[0], rg_wx_2[0]], 0)
    out["w_rg"] = np.ascontiguousarray(rg.transpose(2, 3, 1, 0, 4)).reshape(RNN_BLOCKS, P, 4 * P)
    out["w_out2"] = chunks(w_out_2[0], 4)
    out["w_ffn"] = chunks(w_ffn_in_2[0], 2, [t * KF + n for n in range(KF) for t in range(2)])
    out["w_ffn_out"] = tile_chunks(w_ffn_out_2[0], 1)
    return out


def kernel(**inputs):
    import concourse.bacc as _bacc
    from concourse.bass_utils import run_bass_kernel_spmd as _run

    nc = _bacc.Bacc("TRN2", target_bir_lowering=False, num_devices=1)
    arrays = lay_out(**{k: np.asarray(v) for k, v in inputs.items()})
    io = {name: nc.dram_tensor(f"in_{name}", a.shape, F32, kind="ExternalInput").ap() for name, a in arrays.items()}
    io["out"] = nc.dram_tensor("out_yT", (KD, P, SEQ), F32, kind="ExternalOutput").ap()
    program(nc, io)
    r = _run(nc, [{f"in_{name}": a for name, a in arrays.items()}], core_ids=[0])
    got = r.results[0]["out_yT"]
    return np.ascontiguousarray(got.reshape(1, D, SEQ).transpose(0, 2, 1))
```
